# Optimizing a Trainium2 kernel written in Bass

```python
import functools
import jax, jax.numpy as jnp
from jax import lax
import numpy as np

D_MODEL = 1024
BATCH = 1
SEQ = 1024
DEPTH = 1
DEC_BATCH = 1
DEC_SEQ = 64
PAST_LEN = 256

CHUNK = 64
Q_BLOCK = 128
RET_HEADS = 4
RET_DK = 128
RET_DV = 256
MLA_HEADS = 8
Q_LORA = 512
KV_LORA = 256
NOPE_DIM = 128
ROPE_DIM = 64
V_DIM = 128
D_FF = ((8 * D_MODEL // 3 + 255) // 256) * 256
ROPE_BASE = 10000.0
EPS = 1e-6

RET_QK_W = RET_HEADS * RET_DK
RET_V_W = RET_HEADS * RET_DV
MLA_Q_W = MLA_HEADS * (NOPE_DIM + ROPE_DIM)
MLA_KV_W = MLA_HEADS * (NOPE_DIM + V_DIM)
MLA_V_W = MLA_HEADS * V_DIM
IN_W = 2 * RET_QK_W + 2 * RET_V_W + Q_LORA + KV_LORA + ROPE_DIM + 2 * D_MODEL

kernel_name = "retnet_mla_parallel_gated_stream_step"

def rms_norm(x, g):
    xf = x.astype(jnp.float32)
    y = xf * lax.rsqrt(jnp.mean(xf * xf, axis=-1, keepdims=True) + EPS)
    return (y * g.astype(jnp.float32)).astype(x.dtype)

def rope(x, pos):
    d = x.shape[-1]
    inv = ROPE_BASE ** (-jnp.arange(0, d, 2, dtype=jnp.float32) / d)
    ang = pos.astype(jnp.float32)[:, None] * inv[None, :]
    ang = ang.reshape(ang.shape[:1] + (1,) * (x.ndim - 3) + ang.shape[1:])
    cos, sin = jnp.cos(ang), jnp.sin(ang)
    xf = x.astype(jnp.float32)
    x1, x2 = xf[..., : d // 2], xf[..., d // 2:]
    return jnp.concatenate([x1 * cos - x2 * sin, x1 * sin + x2 * cos], axis=-1).astype(x.dtype)

def split_columns(z):
    sizes = (RET_QK_W, RET_QK_W, RET_V_W, RET_V_W, Q_LORA, KV_LORA, ROPE_DIM, D_MODEL, D_MODEL)
    offs = np.cumsum(sizes)[:-1].tolist()
    return jnp.split(z, offs, axis=-1)

def ret_log_gamma():
    return jnp.log(1.0 - 2.0 ** (-5.0 - jnp.arange(RET_HEADS, dtype=jnp.float32)))

def retention_chunk(state, q, k, v):
    L = q.shape[1]
    lg = ret_log_gamma()
    n = jnp.arange(L, dtype=jnp.float32)
    diff = n[:, None] - n[None, :]
    decay = jnp.where(diff >= 0, jnp.exp(lg[:, None, None] * jnp.maximum(diff, 0.0)), 0.0)
    scores = jnp.einsum('blhd,bmhd->bhlm', q, k) * decay
    inner = jnp.einsum('bhlm,bmhe->blhe', scores, v)
    q_decay = jnp.exp(lg[None, :] * (n[:, None] + 1.0))
    cross = jnp.einsum('blhd,bhde->blhe', q * q_decay[None, :, :, None], state)
    k_decay = jnp.exp(lg[None, :] * (L - 1.0 - n[:, None]))
    new_state = jnp.exp(lg * L)[None, :, None, None] * state + jnp.einsum('blhd,blhe->bhde', k * k_decay[None, :, :, None], v)
    return new_state, inner + cross

def retention_prompt(q, k, v):
    B, S, H, _ = q.shape
    nc = S // CHUNK
    def to_chunks(t):
        return t.astype(jnp.float32).reshape(B, nc, CHUNK, H, t.shape[-1]).swapaxes(0, 1)
    s0 = jnp.zeros((B, H, RET_DK, RET_DV), jnp.float32)
    s_fin, y = lax.scan(lambda s, c: retention_chunk(s, *c), s0, (to_chunks(q), to_chunks(k), to_chunks(v)))
    return y.swapaxes(0, 1).reshape(B, S, H, RET_DV), s_fin

def head_group_norm(y, g):
    mu = jnp.mean(y, axis=-1, keepdims=True)
    yc = y - mu
    yn = yc * lax.rsqrt(jnp.mean(yc * yc, axis=-1, keepdims=True) + EPS)
    B, S = y.shape[:2]
    return yn.reshape(B, S, RET_V_W) * g.astype(jnp.float32)

def mla_decompress(ckv, w_ukv):
    B, T, _ = ckv.shape
    kv = (ckv @ w_ukv).reshape(B, T, MLA_HEADS, NOPE_DIM + V_DIM)
    return kv[..., :NOPE_DIM], kv[..., NOPE_DIM:]

def mla_attend(q, k_nope, kpe, v, mask):
    scale = (NOPE_DIM + ROPE_DIM) ** -0.5
    s = (jnp.einsum('bqhd,bkhd->bhqk', q[..., :NOPE_DIM], k_nope).astype(jnp.float32)
         + jnp.einsum('bqhr,bkr->bhqk', q[..., NOPE_DIM:], kpe).astype(jnp.float32)) * scale
    s = jnp.where(mask, s, jnp.finfo(jnp.float32).min)
    p = jax.nn.softmax(s, axis=-1)
    return jnp.einsum('bhqk,bkhe->bqhe', p.astype(v.dtype), v)

def mla_prompt(q, ckv, kpe, w_ukv):
    B, S = q.shape[:2]
    k_nope, v = mla_decompress(ckv, w_ukv)
    nb = S // Q_BLOCK
    qb = q.reshape(B, nb, Q_BLOCK, MLA_HEADS, NOPE_DIM + ROPE_DIM).swapaxes(0, 1)
    key_chunk = jnp.arange(S) // CHUNK
    def one_block(args):
        qi, i = args
        q_chunk = (i * Q_BLOCK + jnp.arange(Q_BLOCK)) // CHUNK
        mask = key_chunk[None, :] <= q_chunk[:, None]
        return mla_attend(qi, k_nope, kpe, v, mask)
    out = lax.map(one_block, (qb, jnp.arange(nb)))
    return out.swapaxes(0, 1).reshape(B, S, MLA_V_W)

def prompt_core(rq, rk, rv, q, ckv, kpe, w_ukv):
    ret_y, s_fin = retention_prompt(rq, rk, rv)
    mla_y = mla_prompt(q, ckv, kpe, w_ukv)
    return ret_y, mla_y, (ckv, kpe, s_fin.astype(ckv.dtype))

def sample_core(cache_ckv, cache_kpe, state_ret, rq, rk, rv, q, ckv, kpe, w_ukv):
    f32 = jnp.float32
    B, L = q.shape[:2]
    s_new, ret_y = retention_chunk(state_ret.astype(f32), rq.astype(f32), rk.astype(f32), rv.astype(f32))
    keys_ckv = jnp.concatenate([cache_ckv.astype(ckv.dtype), ckv], axis=1)
    keys_kpe = jnp.concatenate([cache_kpe.astype(kpe.dtype), kpe], axis=1)
    k_nope, v = mla_decompress(keys_ckv, w_ukv)
    mask = jnp.ones((L, keys_ckv.shape[1]), dtype=bool)
    mla_y = mla_attend(q, k_nope, keys_kpe, v, mask).reshape(B, L, MLA_V_W)
    return ret_y, mla_y, (ckv, kpe, s_new.astype(state_ret.dtype))

def layer_forward(x, pos, mixer_core, norm_mix_w, w_in, q_norm_w, w_uq, kv_norm_w, w_ukv,
                  ret_gn_w, w_ret_o, w_mla_o, w_out, norm_ffn_w, w_gate_up, w_down):
    B, S, _ = x.shape
    xn = rms_norm(x, norm_mix_w)
    rq, rk, rv, rg, cq, ckv, kpe, ga, gb = split_columns(xn @ w_in)
    rq = rope(rq.reshape(B, S, RET_HEADS, RET_DK), pos)
    rk = rope(rk.reshape(B, S, RET_HEADS, RET_DK), pos) * (RET_DK ** -0.5)
    rv = rv.reshape(B, S, RET_HEADS, RET_DV)
    q = (rms_norm(cq, q_norm_w) @ w_uq).reshape(B, S, MLA_HEADS, NOPE_DIM + ROPE_DIM)
    q = jnp.concatenate([q[..., :NOPE_DIM], rope(q[..., NOPE_DIM:], pos)], axis=-1)
    ckv = rms_norm(ckv, kv_norm_w)
    kpe = rope(kpe, pos)
    ret_y, mla_y, new_state = mixer_core(rq, rk, rv, q, ckv, kpe, w_ukv)
    ret_branch = (head_group_norm(ret_y, ret_gn_w).astype(x.dtype) * jax.nn.silu(rg)) @ w_ret_o
    mla_branch = mla_y @ w_mla_o
    merged = jax.nn.sigmoid(ga) * ret_branch + jax.nn.sigmoid(gb) * mla_branch
    h = x + merged @ w_out
    g, u = jnp.split(rms_norm(h, norm_ffn_w) @ w_gate_up, 2, axis=-1)
    h = h + (jax.nn.silu(g) * u) @ w_down
    return h, new_state

def setup_inputs(seed: int = 0) -> dict:
    key = jax.random.key(seed)
    ks = jax.random.split(key, 24)
    f32 = jnp.float32
    def w(k, shape, fan_in):
        return jax.random.normal(k, shape, f32) * fan_in ** -0.5
    def gain(k, shape):
        return 1.0 + 0.02 * jax.random.normal(k, shape, f32)
    return {
        "x_prompt": jax.random.normal(ks[0], (BATCH, SEQ, D_MODEL), f32),
        "x_sample": jax.random.normal(ks[1], (DEC_BATCH, DEC_SEQ, D_MODEL), f32),
        "cache_ckv": jax.random.normal(ks[2], (DEPTH, DEC_BATCH, PAST_LEN, KV_LORA), f32),
        "cache_kpe": jax.random.normal(ks[3], (DEPTH, DEC_BATCH, PAST_LEN, ROPE_DIM), f32),
        "state_ret": 0.5 * jax.random.normal(ks[4], (DEPTH, DEC_BATCH, RET_HEADS, RET_DK, RET_DV), f32),
        "norm_mix_w": gain(ks[5], (DEPTH, D_MODEL)),
        "w_in": w(ks[6], (DEPTH, D_MODEL, IN_W), D_MODEL),
        "q_norm_w": gain(ks[7], (DEPTH, Q_LORA)),
        "w_uq": w(ks[8], (DEPTH, Q_LORA, MLA_Q_W), Q_LORA),
        "kv_norm_w": gain(ks[9], (DEPTH, KV_LORA)),
        "w_ukv": w(ks[10], (DEPTH, KV_LORA, MLA_KV_W), KV_LORA),
        "ret_gn_w": gain(ks[11], (DEPTH, RET_V_W)),
        "w_ret_o": w(ks[12], (DEPTH, RET_V_W, D_MODEL), RET_V_W),
        "w_mla_o": w(ks[13], (DEPTH, MLA_V_W, D_MODEL), MLA_V_W),
        "w_out": w(ks[14], (DEPTH, D_MODEL, D_MODEL), D_MODEL),
        "norm_ffn_w": gain(ks[15], (DEPTH, D_MODEL)),
        "w_gate_up": w(ks[16], (DEPTH, D_MODEL, 2 * D_FF), D_MODEL),
        "w_down": w(ks[17], (DEPTH, D_FF, D_MODEL), D_FF),
        "norm_final_w": gain(ks[18], (D_MODEL,)),
    }

def reference(x_prompt, x_sample, cache_ckv, cache_kpe, state_ret, norm_mix_w, w_in, q_norm_w, w_uq,
              kv_norm_w, w_ukv, ret_gn_w, w_ret_o, w_mla_o, w_out, norm_ffn_w, w_gate_up, w_down, norm_final_w):
    past = cache_ckv.shape[2]
    pos_p = jnp.arange(x_prompt.shape[1])
    pos_s = past + jnp.arange(x_sample.shape[1])
    hp, hs = x_prompt, x_sample
    p_ckv, p_kpe, p_ret, s_ckv, s_kpe, s_ret = [], [], [], [], [], []
    for l in range(DEPTH):
        lw = (norm_mix_w[l], w_in[l], q_norm_w[l], w_uq[l], kv_norm_w[l], w_ukv[l], ret_gn_w[l],
              w_ret_o[l], w_mla_o[l], w_out[l], norm_ffn_w[l], w_gate_up[l], w_down[l])
        hp, (a, b, c) = layer_forward(hp, pos_p, prompt_core, *lw)
        core = functools.partial(sample_core, cache_ckv[l], cache_kpe[l], state_ret[l])
        hs, (d, e, f) = layer_forward(hs, pos_s, core, *lw)
        p_ckv.append(a); p_kpe.append(b); p_ret.append(c)
        s_ckv.append(d); s_kpe.append(e); s_ret.append(f)
    y_prompt = rms_norm(hp, norm_final_w)
    y_sample = rms_norm(hs, norm_final_w)
    return (y_prompt, y_sample, jnp.stack(p_ckv), jnp.stack(p_kpe), jnp.stack(p_ret),
            jnp.stack(s_ckv), jnp.stack(s_kpe), jnp.stack(s_ret))


_drawn_inputs = setup_inputs


def setup_inputs(seed=0):
    import zlib

    import numpy as np

    out = dict(_drawn_inputs(seed))
    spreads = {}
    factors = {'q_norm_w': 8.0,
     'kv_norm_w': 2.734,
     'ret_gn_w': 8.0,
     'norm_ffn_w': 4.03,
     'norm_final_w': 8.358,
     'cache_ckv': 2.794,
     'cache_kpe': 3.891}
    for name, (base, spread) in spreads.items():
        noise = np.random.default_rng([zlib.crc32(name.encode()), seed]).standard_normal(out[name].shape)
        drawn = base * np.exp(spread * noise) if base else spread * noise
        out[name] = __import__('jax').numpy.asarray(drawn.astype(out[name].dtype))
    for name, factor in factors.items():
        out[name] = (out[name] * factor).astype(out[name].dtype)
    return out
```

```python
from contextlib import ExitStack

import concourse.bass as bass
from concourse import mybir

F32 = mybir.dt.float32
F32R = mybir.dt.float32r
ALU = mybir.AluOpType
ACT = mybir.ActivationFunctionType
AX = mybir.AxisListType

P = 128
D_MODEL = 1024
SEQ = 1024
DEC = 64
PAST = 256
TOK = SEQ + DEC
KEYS = TOK + PAST
RH, DK, DV = 4, 128, 256
MH = 8
Q_LORA, KV_LORA, NOPE, ROPE, VD = 512, 256, 128, 64, 128
D_FF = ((8 * D_MODEL // 3 + 255) // 256) * 256
EPS = 1e-6
KT = D_MODEL // P
GROUPS = ((0, 384), (384, 768), (768, 1088))
KEY_GROUPS = ((0, 448), (448, 896), (896, 1344))
NG = 3
WIDE = 384
FT = D_FF // P
FFN_GROUPS = ((0, 8), (8, 8), (16, 6))
U = TOK * 4
SCALE = float(NOPE + ROPE) ** -0.5
NEG = -3.0e38

N_A = 7
N_MLA = 12
N_RET = 4 * RH
I_A = 0
I_MLA = I_A + N_A
I_RET = I_MLA + N_MLA
I_GATE = I_RET + N_RET
I_M1 = I_GATE + 8
I_M2 = I_M1 + 16
I_OUT = I_M2 + 16
I_FFN = I_OUT + 8
N_ITEMS = I_FFN + sum(2 * n + 8 for _, n in FFN_GROUPS)

G_A = 0
G_GATE = G_A + 3 * N_A
G_M1 = G_GATE + 3 * 8
G_M2 = G_M1 + 3 * 16
G_OUT = G_M2 + 3 * 16
G_FFN = G_OUT + 3 * 8


def attention_steps(head):
    order = [8, 0, 1, 2, 3, 4, 5, 6, 7]
    fill = []
    if head + 1 < MH:
        fill = [("F", head + 1, kind, g) for kind in "KVQ" for g in range(NG)]
        if head % 2:
            fill += [("F", head + 1, "R", g) for g in range(NG)]
    steps = [("S", 8), ("S", 0)]
    for k, tile in enumerate(order):
        if fill:
            steps.append(fill.pop(0))
        steps.append(("T", tile))
        if tile == 8:
            steps.append(("O", 4))
        elif tile % 2:
            steps.append(("O", tile // 2))
        if k + 2 < len(order):
            steps.append(("S", order[k + 2]))
    return steps + fill


def retention_steps(head):
    fill = []
    if head + 1 < RH:
        fill = [("F", head + 1, kind, g) for kind in "QK" for g in range(NG)]
        fill += [("F", head + 1, "V", t) for t in range(9)]
    steps = []
    for c in range(9):
        steps.append(("C", c))
        for _ in range(2):
            if fill:
                steps.append(fill.pop(0))
        steps.append(("Z", c))
    return steps + fill


def keys_of(tile):
    return (0, (tile + 1) * P, P) if tile < 8 else (SEQ, DEC + PAST, DEC)


def build(nc, a, o):
    with ExitStack() as ctx:
        base = (nc.sbuf_base + 63) // 64 * 64

        def at(name, offset, shape, dt=F32):
            return nc.alloc_sbuf_tensor_at(name, [P, *shape], dt, offset=base + offset)

        def sem(name):
            return ctx.enter_context(nc.semaphore(name))

        stage = [at(f"w_stage{s}", 4096 * s, [8, P]) for s in range(2)]
        w_hi = at("w_hi", 8192, [2, 8, P], F32R)
        w_lo = at("w_lo", 16384, [2, 8, P], F32R)
        TMP = 24576
        tmp = [at(f"tmp{k}", TMP + WIDE * 4 * k, [WIDE]) for k in range(6)]
        CON = TMP + 6 * WIDE * 4
        eye = at("eye", CON, [P])
        ones = at("ones", CON + 512, [P])
        gains = at("gains", CON + 1024, [38])
        eps = at("eps", CON + 1216, [1])
        negmax = at("negmax", CON + 1280, [2, 2])
        rowsum = at("rowsum", CON + 1344, [2, 2])
        bnst = at("bnst", CON + 1408, [2, 6])
        mv = at("mv", CON + 1472, [2, 2])
        rstd = at("rstd", CON + 1536, [2, 1])
        half = at("half", CON + 1600, [1])
        veps = at("veps", CON + 1632, [2, 1])
        G_MIX, G_Q, G_KV, G_GN, G_F, G_FIN = 0, 8, 12, 14, 22, 30
        M = CON + 4096

        def region(name, units, shape, dt=F32, extra=0):
            return at(name, M + int(units * U) + extra, shape, dt)

        xn_hi = region("xn_hi", 0, [KT, TOK], F32R)
        xn_lo = region("xn_lo", 8, [KT, TOK], F32R)
        xt = region("xt", 16, [KT, TOK])
        square = region("square", 0, [2, TOK])
        square_late = region("square_late", 16, [2, TOK])
        sumsq = region("sumsq", 30, [TOK])
        inv = region("inv", 31, [TOK])
        cq_raw = region("cq_raw", 32, [4, TOK])
        ckv_raw = region("ckv_raw", 36, [2, TOK])
        kpe_out = region("kpe_out", 38, [TOK])
        kp_hi = region("kp_hi", 25.25, [KEYS], F32R)
        kp_lo = region("kp_lo", 25.25, [KEYS], F32R, extra=KEYS * 4)
        cos64 = region("cos64", 27.75, [TOK])
        sin64 = region("sin64", 28.75, [TOK])
        cqn_hi = region("cqn_hi", 0, [4, TOK], F32R)
        cqn_lo = region("cqn_lo", 4, [4, TOK], F32R)
        ckn_hi = region("ckn_hi", 8, [2, KEYS], F32R)
        ckn_lo = region("ckn_lo", 8, [2, KEYS], F32R, extra=2 * KEYS * 4)
        cache_in = region("cache_in", 18, [2, PAST])
        cpe_in = region("cpe_in", 18, [PAST], extra=2 * PAST * 4)
        K_B, V_B = KEYS * 4, 11 * VD * 4
        k_hi = [region(f"k_hi{b}", 13, [KEYS], F32R, extra=2 * b * K_B) for b in range(2)]
        k_lo = [region(f"k_lo{b}", 13, [KEYS], F32R, extra=(2 * b + 1) * K_B) for b in range(2)]
        v_hi = [region(f"v_hi{b}", 18, [11, VD], F32R, extra=2 * b * V_B) for b in range(2)]
        v_lo = [region(f"v_lo{b}", 18, [11, VD], F32R, extra=(2 * b + 1) * V_B) for b in range(2)]
        p_exp = [region(f"p_exp{b}", 23.25, [SEQ], extra=4096 * b) for b in range(2)]
        q_hi = [region(f"q_hi{b}", 29.75 + 2 * b, [TOK], F32R) for b in range(2)]
        q_lo = [region(f"q_lo{b}", 30.75 + 2 * b, [TOK], F32R) for b in range(2)]
        qr = [region(f"qr{b}", 33.75 + b, [TOK], F32R) for b in range(2)]
        pt_hi = region("pt_hi", 36, [8, 2 * P], F32R)
        pt_lo = region("pt_lo", 36, [8, 2 * P], F32R, extra=8192)
        out_hl = [at(f"out_hl{b}", TMP + 5120 + 2048 * b, [2, 2 * P], F32R) for b in range(2)]
        rq_hi = [region(f"rq_hi{b}", 16 + b, [TOK], F32R) for b in range(2)]
        rq_lo = [region(f"rq_lo{b}", 18 + b, [TOK], F32R) for b in range(2)]
        rk_hi = [region(f"rk_hi{b}", 20 + b, [TOK], F32R) for b in range(2)]
        rk_lo = [region(f"rk_lo{b}", 22 + b, [TOK], F32R) for b in range(2)]
        rk_f = [region(f"rk_f{b}", 24 + b, [TOK]) for b in range(2)]
        RV_B = 9 * DV * 4
        rv_hi = [region(f"rv_hi{b}", 26, [9, DV], F32R, extra=2 * b * RV_B) for b in range(2)]
        rv_lo = [region(f"rv_lo{b}", 26, [9, DV], F32R, extra=(2 * b + 1) * RV_B) for b in range(2)]
        cos128 = region("cos128", 34.5, [TOK])
        sin128 = region("sin128", 35.5, [TOK])
        R0 = int(36.5 * U)
        dmask = region("dmask", 0, [RH, P], extra=R0)
        dcol = region("dcol", 0, [RH, 3], extra=R0 + 2048)
        st_f = region("st_f", 0, [P], extra=R0 + 2112)
        st_hi = region("st_hi", 0, [P], F32R, extra=R0 + 2624)
        st_lo = region("st_lo", 0, [P], F32R, extra=R0 + 3136)
        kd_hi = region("kd_hi", 0, [P], F32R, extra=R0 + 3648)
        kd_lo = region("kd_lo", 0, [P], F32R, extra=R0 + 4160)
        s_f = region("s_f", 0, [DV], extra=R0 + 4672)
        s_hi = region("s_hi", 0, [DV], F32R, extra=R0 + 5696)
        s_lo = region("s_lo", 0, [DV], F32R, extra=R0 + 6720)
        zs = region("zs", 0, [DV], extra=R0 + 7744)
        zn = [region(f"zn{b}", 0, [DV], extra=R0 + 8768 + 1024 * b) for b in range(2)]
        zt = [region(f"zt{b}", 0, [2, P], extra=R0 + 10816 + 1024 * b) for b in range(2)]
        s_in = region("s_in", 0, [DV], extra=R0 + 12864)
        y_hi = region("y_hi", 16, [8, TOK], F32R)
        y_lo = region("y_lo", 24, [8, TOK], F32R)
        res = region("res", 32, [8, TOK])
        res_sq = region("res_sq", 22, [TOK])
        res_inv = region("res_inv", 23, [TOK])
        norm_f = [region(f"norm_f{b}", 18 + b, [TOK]) for b in range(2)]

        ps = ctx.enter_context(nc.psum_tensor("ps", [P, 8, 512], F32))

        xn_spill = nc.dram_tensor("xn_spill", (P, 2, KT, TOK), F32, kind="Internal").ap()
        ym_spill = nc.dram_tensor("ym_spill", (MH, P, 2, TOK), F32, kind="Internal").ap()
        yr_spill = nc.dram_tensor("yr_spill", (8, P, TOK), F32, kind="Internal").ap()

        stage_in = [sem("stage_in0"), sem("stage_in1")]
        w_high = sem("w_high")
        w_low = sem("w_low")
        consts_in = sem("consts_in")
        x_in = [sem(f"x_in{t}") for t in range(KT)]
        tables_in = sem("tables_in")
        cache_landed = sem("cache_landed")
        cache_high = sem("cache_high")
        cache_low = sem("cache_low")
        kv_out = sem("kv_out")
        set_up = sem("set_up")
        squared = sem("squared")
        summed = sem("summed")
        stat_done = sem("stat_done")
        root_done = sem("root_done")
        inv_done = sem("inv_done")
        scaled = sem("scaled")
        norm_high = sem("norm_high")
        norm_low = sem("norm_low")
        g_done = sem("g_done")
        g_act = sem("g_act")
        g_free = sem("g_free")
        g_high = sem("g_high")
        g_low = sem("g_low")
        p_done = sem("p_done")
        p_high = sem("p_high")
        p_free = sem("p_free")
        rot_sum = sem("rot_sum")
        rot_high = sem("rot_high")
        rot_low = sem("rot_low")
        v_chain = sem("v_chain")
        pool_chain = sem("pool_chain")
        s_done = sem("s_done")
        max_done = sem("max_done")
        exp_done = sem("exp_done")
        prob_done = sem("prob_done")
        t_done = sem("t_done")
        t_high = sem("t_high")
        t_low = sem("t_low")
        o_out = [sem("o_out0"), sem("o_out1")]
        kd_done = sem("kd_done")
        kd_high = sem("kd_high")
        kd_low = sem("kd_low")
        sc_done = sem("sc_done")
        sc_mid = sem("sc_mid")
        sc_high = sem("sc_high")
        sc_low = sem("sc_low")
        z_done = sem("z_done")
        z_copy = sem("z_copy")
        z_stat = sem("z_stat")
        z_rstd = sem("z_rstd")
        z_norm = sem("z_norm")
        zt_done = sem("zt_done")
        zt_copy = sem("zt_copy")
        zt_out = [sem("zt_out0"), sem("zt_out1")]
        u_done = sem("u_done")
        state_load = sem("state_load")
        state_f = sem("state_f")
        state_high = sem("state_high")
        state_low = sem("state_low")
        state_in = sem("state_in")
        state_out = sem("state_out")
        spill_out = sem("spill_out")
        xn_in = [sem(f"xn_in{t}") for t in range(KT)]
        yr_in = [sem("yr_in0"), sem("yr_in1")]
        ym_in = [sem(f"ym_in{t}") for t in range(KT)]
        m_add = sem("m_add")
        split_hi = sem("split_hi")
        split_lo = sem("split_lo")
        xres_in = [sem("xres_in0"), sem("xres_in1")]
        out_done = sem("out_done")

        W = a["weights"]
        def s_index(h, tile):
            return 9 * h + (0 if tile == 8 else tile + 1)

        T_UNITS = [1] + [t // 4 + 1 for t in range(8)]
        T_HEAD = sum(T_UNITS)

        def t_index(h, tile):
            pos = 0 if tile == 8 else tile + 1
            return T_HEAD * h + sum(T_UNITS[:pos])

        def t_blocks(tile):
            n = tile + 1 if tile < 8 else 3
            return [(k, min(4, n - k)) for k in range(0, n, 4)]

        def o_index(h, pair):
            return 5 * h + (0 if pair == 4 else pair + 1)

        p_order = {}
        for h in range(MH):
            if h == 0:
                for kind in "KVQR":
                    for g in range(NG):
                        p_order["M", 0, kind, g] = len(p_order)
            for s in attention_steps(h):
                if s[0] == "F":
                    p_order["M", *s[1:]] = len(p_order)
                if s[0] == "O":
                    p_order["M", h, "O", s[1]] = len(p_order)
        P_MLA = len(p_order)
        for h in range(RH):
            if h == 0:
                for kind, count in (("Q", NG), ("K", NG), ("V", 9)):
                    for g in range(count):
                        p_order["R", 0, kind, g] = len(p_order)
            for s in retention_steps(h):
                if s[0] == "F":
                    p_order["R", *s[1:]] = len(p_order)
        P_ALL = len(p_order)
        rotated = [k for k in p_order if (k[0] == "M" and k[2] == "R") or (k[0] == "R" and k[2] in "QK")]
        rot_index = {k: i + NG for i, k in enumerate(rotated)}

        def t_end(n):
            return T_HEAD * (n // 9) + sum(T_UNITS[:n % 9 + 1])

        F_A, F_GATE = 0, 3 * N_A
        F_M1, A_M1 = F_GATE + 24, 24
        F_M2, A_M2 = F_M1 + 24, A_M1 + 24
        F_OUT, F_FFN, A_FFN = F_M2 + 24, F_M2 + 48, A_M2 + 24
        SUM_OUT, SUM_FIN = KT + 6, KT + 6 + 24

        def mla_item(h, kind):
            pair = I_MLA + 3 * (h // 2)
            if kind == "R":
                return pair + 1
            return pair + (2 if h % 2 else 0)

        def ret_item(h, kind):
            return I_RET + 4 * h + {"Q": 0, "K": 1, "V": 2}[kind]

        rot_cos, rot_sin, rot_total = tmp[0], tmp[1], tmp[2]
        root = tmp[3]

        block = ctx.enter_context(nc.Block())

        @block.sync
        def _(sp):
            def load_item(n):
                sp.dma_start(stage[n % 2][:, :, :], W[n]).then_inc(stage_in[n % 2], 16)

            def items(first, last):
                for n in range(first, last):
                    sp.wait_ge(w_low, n - 1)
                    load_item(n)

            def item_in_loop(i, n):
                sp.wait_ge(w_low, 2 * i + (n - 1))
                sp.dma_start(stage[n % 2][:, :, :], W[2 * i + n]).then_inc(stage_in[n % 2], 16)

            for t in range(KT):
                sp.dma_start(xt[:, t, :], a["x"][:, t, :]).then_inc(x_in[t], 16)
            for name, dst in (("eye", eye[:, :]), ("gains", gains[:, :])):
                sp.dma_start(dst, a[name]).then_inc(consts_in, 16)
            load_item(0)
            load_item(1)
            sp.dma_start(cos64[:, :], a["cos64"]).then_inc(tables_in, 16)
            sp.dma_start(sin64[:, :], a["sin64"]).then_inc(tables_in, 16)
            for t in range(KT):
                sp.wait_ge(norm_low, t + 1)
                sp.dma_start(xn_spill[:, 0, t, :], xn_hi[:, t, :].bitcast(F32)).then_inc(spill_out, 16)
                sp.dma_start(xn_spill[:, 1, t, :], xn_lo[:, t, :].bitcast(F32)).then_inc(spill_out, 16)
            sp.dma_start(cache_in[:, :, :], a["cache_ckv"]).then_inc(cache_landed, 16)
            sp.dma_start(cpe_in[0:ROPE, :], a["cache_kpe"]).then_inc(cache_landed, 16)
            items(2, I_MLA + 2)
            sp.wait_ge(rot_sum, NG)
            sp.dma_start(o["kpe"], kpe_out[0:ROPE, 0:TOK]).then_inc(kv_out, 16)
            sp.wait_ge(scaled, KT + 2)
            sp.dma_start(o["ckv"], ckv_raw[:, :, :]).then_inc(kv_out, 16)
            items(I_MLA + 2, I_MLA + 4)
            for h in range(MH):
                for s in attention_steps(h):
                    if s[0] == "F" and s[3] == 0 and s[2] in "KR":
                        n = mla_item(s[1], s[2]) + 2
                        items(n, n + 1)
                    if s[0] == "O":
                        n = o_index(h, s[1])
                        c0, c1 = (SEQ, TOK) if s[1] == 4 else (s[1] * 2 * P, (s[1] + 1) * 2 * P)
                        sp.wait_ge(p_free, p_order["M", h, "O", s[1]] + 1)
                        sp.dma_start(ym_spill[h, :, :, c0:c1],
                                     out_hl[n % 2][:, :, 0:c1 - c0].bitcast(F32)).then_inc(o_out[n % 2], 16)
            sp.wait_ge(spill_out, 2 * KT * 16)
            sp.wait_ge(p_free, P_MLA)
            for t in range(KT):
                sp.dma_start(xn_hi[:, t, :].bitcast(F32), xn_spill[:, 0, t, :]).then_inc(xn_in[t], 16)
                sp.dma_start(xn_lo[:, t, :].bitcast(F32), xn_spill[:, 1, t, :]).then_inc(xn_in[t], 16)
            for name, dst in (("cos128", cos128[:, :]), ("sin128", sin128[:, :]),
                              ("dmask", dmask[:, :, :]), ("dcol", dcol[:, :, :])):
                sp.dma_start(dst, a[name]).then_inc(tables_in, 16)
            items(I_RET + 2, I_RET + 6)
            for h in range(RH):
                for s in retention_steps(h):
                    if s[0] == "F" and s[3] == 0:
                        n = ret_item(s[1], s[2]) + 2
                        items(n, n + (2 if s[2] == "V" else 1))
                    if s == ("C", 8):
                        sp.wait_ge(state_f, 9 * h + 8)
                        sp.dma_start(o["state_p"][:, h, :], s_f[:, :]).then_inc(state_out, 16)
                        if h:
                            sp.wait_ge(state_load, 2 * h)
                        sp.dma_start(s_in[:, :], a["state"][:, h, :]).then_inc(state_in, 16)
                    if s[0] == "Z":
                        n = 9 * h + s[1]
                        c0, c1 = s[1] * P, min(TOK, (s[1] + 1) * P)
                        sp.wait_ge(zt_copy, n + 1)
                        for j in range(2):
                            sp.dma_start(yr_spill[2 * h + j, :, c0:c1],
                                         zt[n % 2][:, j, 0:c1 - c0]).then_inc(zt_out[n % 2], 16)
                sp.wait_ge(state_f, 9 * h + 9)
                sp.dma_start(o["state_s"][:, h, :], s_f[:, :]).then_inc(state_out, 16)
            for b in range(2):
                sp.wait_ge(zt_out[b], 32 * 18)
            sp.wait_ge(rot_low, NG + len(rotated))
            with sp.Fori(0, 4) as i:
                for j in range(2):
                    for g, (c0, c1) in enumerate(GROUPS):
                        k = 3 * j + g
                        sp.wait_ge(g_free, 6 * i + (F_GATE + k - 1))
                        sp.dma_start(tmp[k % 2][:, 0:c1 - c0], yr_spill[2 * i + j, :, c0:c1])\
                          .then_inc(yr_in[k % 2], 16)
                    item_in_loop(i, I_GATE + 2 + j)
            with sp.Fori(0, 8) as i:
                for j in range(2):
                    item_in_loop(i, I_M1 + 2 + j)
            for b in range(2):
                sp.wait_ge(o_out[b], 16 * 20)
            sp.wait_ge(g_done, G_M2)
            for t in range(KT):
                sp.dma_start(y_hi[:, t, :].bitcast(F32), ym_spill[t, :, 0, :]).then_inc(ym_in[t], 16)
                sp.dma_start(y_lo[:, t, :].bitcast(F32), ym_spill[t, :, 1, :]).then_inc(ym_in[t], 16)
            with sp.Fori(0, 8) as i:
                for j in range(2):
                    item_in_loop(i, I_M2 + 2 + j)
            with sp.Fori(0, 4) as i:
                for j in range(2):
                    for g, (c0, c1) in enumerate(GROUPS):
                        k = 3 * j + g
                        sp.wait_ge(g_free, 6 * i + (F_OUT + k - 1))
                        sp.dma_start(tmp[k % 2][:, 0:c1 - c0], a["x"][:, 2 * i + j, c0:c1])\
                          .then_inc(xres_in[k % 2], 16)
                    item_in_loop(i, I_OUT + 2 + j)
            with sp.Fori(0, (N_ITEMS - I_FFN) // 2 - 1) as i:
                for j in range(2):
                    item_in_loop(i, I_FFN + 2 + j)
            for t in range(KT):
                sp.wait_ge(scaled, 2 * KT + 6 + t + 1)
                sp.dma_start(o["y"][:, t, :], res[:, t, :]).then_inc(out_done, 16)
            sp.wait_ge(state_out, 16 * 2 * RH)
            sp.wait_ge(kv_out, 32)
            sp.wait_ge(out_done, 16 * KT)

        @block.tensor
        def _(pe):
            def product(out, wh, wl, xh, xl, start=True, stop=True):
                nc.tensor.matmul(out, wh, xh, start=start, stop=False)
                nc.tensor.matmul(out, wl, xh, start=False, stop=False)
                return nc.tensor.matmul(out, wh, xl, start=False, stop=stop)

            def item_units(slot, n, bank, free, hi, lo, blocks=8, rows=P, ready=None):
                pe.wait_ge(w_low, n + 1)
                for g, (c0, c1) in enumerate(GROUPS):
                    if free is not None:
                        pe.wait_ge(free[0], free[1] + g)
                    out = ps[0:rows, bank + g, 0:c1 - c0]
                    for k in range(blocks):
                        if ready is not None and g == 0:
                            ready(k)
                        last = product(out, w_hi[:, slot, k, 0:rows], w_lo[:, slot, k, 0:rows],
                                       hi[:, k, c0:c1], lo[:, k, c0:c1], k == 0, k == blocks - 1)
                    last.then_inc(g_done, 1)

            def feature_sums(k, src):
                for g, (c0, c1) in enumerate(GROUPS):
                    if k or g:
                        pe.wait_ge(root_done, 3 * k + g)
                    nc.tensor.matmul(ps[:, 7, 0:c1 - c0], ones[:, :], src[:, c0:c1],
                                     start=True, stop=True).then_inc(stat_done, 1)

            pe.wait_ge(summed, KT)
            feature_sums(0, sumsq)
            for j in range(N_A):
                n = I_A + j
                ready = (lambda k: pe.wait_ge(norm_low, k + 1)) if j == 0 else None
                item_units(n % 2, n, 3 * (j % 2), None if j < 2 else (g_free, 3 * j - 5), xn_hi, xn_lo,
                           rows=ROPE if j == N_A - 1 else P, ready=ready)
            pe.wait_ge(summed, KT + 2)
            feature_sums(1, sumsq)
            pe.wait_ge(summed, KT + 6)
            feature_sums(2, sumsq)

            def projection(h, kind, g):
                b, key = h % 2, ("M", h, kind, g)
                u = p_order[key]
                bank = 6 + u % 2
                n = mla_item(h, kind)
                slot = n % 2
                pe.wait_ge(w_low, n + 1)
                if u >= 2:
                    pe.wait_ge(p_free, u - 1)
                if kind == "K":
                    c0, c1 = KEY_GROUPS[g]
                    for k in range(2):
                        last = product(ps[:, bank, 0:c1 - c0], w_hi[:, slot, k, :], w_lo[:, slot, k, :],
                                       ckn_hi[:, k, c0:c1], ckn_lo[:, k, c0:c1], k == 0, k == 1)
                elif kind == "V":
                    for t in range(4 * g, min(11, 4 * g + 4)):
                        c0, c1 = t * P, min(KEYS, (t + 1) * P)
                        for k in range(2):
                            last = product(ps[0:c1 - c0, bank, (t % 4) * P:(t % 4 + 1) * P],
                                           ckn_hi[:, k, c0:c1], ckn_lo[:, k, c0:c1],
                                           w_hi[:, slot, 2 + k, :], w_lo[:, slot, 2 + k, :], k == 0, k == 1)
                else:
                    c0, c1 = GROUPS[g]
                    first = 4 if kind == "Q" else 0
                    for k in range(4):
                        last = product(ps[:, bank, 0:c1 - c0], w_hi[:, slot, first + k, :],
                                       w_lo[:, slot, first + k, :],
                                       cqn_hi[:, k, c0:c1], cqn_lo[:, k, c0:c1], k == 0, k == 3)
                last.then_inc(p_done, 1)

            pe.wait_ge(norm_low, KT + 6)
            pe.wait_ge(cache_low, 1)
            pe.wait_ge(rot_low, NG)
            pe.wait_ge(root_done, 9)
            pe.wait_ge(g_free, F_GATE)
            for kind in "KVQR":
                for g in range(NG):
                    projection(0, kind, g)
            for h in range(MH):
                b = h % 2
                for s in attention_steps(h):
                    if s[0] == "F":
                        projection(*s[1:])
                    elif s[0] == "S":
                        tile = s[1]
                        n = s_index(h, tile)
                        key0, nk, nq = keys_of(tile)
                        if s[1] == 8:
                            if h % 2 == 0:
                                pe.wait_ge(rot_low, 1 + rot_index["M", h, "R", NG - 1])
                            pe.wait_ge(p_free, 1 + p_order["M", h, "Q", NG - 1])
                        if n >= 2:
                            pe.wait_ge(exp_done, n - 1)
                        q0 = tile * P
                        for c in range(0, nk, 512):
                            w = min(512, nk - c)
                            out = ps[0:nq, 2 * (n % 2) + c // 512, 0:w]
                            keys = slice(key0 + c, key0 + c + w)
                            product(out, q_hi[b][:, q0:q0 + nq], q_lo[b][:, q0:q0 + nq],
                                    k_hi[b][:, keys], k_lo[b][:, keys], True, False)
                            nc.tensor.matmul(out, qr[b][:, q0:q0 + nq], kp_hi[:, keys], start=False, stop=False)
                            last = nc.tensor.matmul(out, qr[b][:, q0:q0 + nq], kp_lo[:, keys],
                                                    start=False, stop=True)
                        last.then_inc(s_done, 1)
                    elif s[0] == "T":
                        tile = s[1]
                        n = s_index(h, tile)
                        _, nk, nq = keys_of(tile)
                        pe.wait_ge(prob_done, n + 1)
                        for i, (k0, nb) in enumerate(t_blocks(tile)):
                            t = t_index(h, tile) + i
                            if t >= 2:
                                pe.wait_ge(t_low, t - 1)
                            for k in range(nb):
                                w = min(P, nk - (k0 + k) * P)
                                last = nc.tensor.transpose(
                                    ps[0:w, 4 + t % 2, k * P:k * P + nq],
                                    p_exp[n % 2][0:nq, (k0 + k) * P:(k0 + k) * P + w], eye[0:nq, 0:nq])
                            last.then_inc(t_done, 1)
                    else:
                        pair = s[1]
                        u = p_order["M", h, "O", pair]
                        pe.wait_ge(t_low, t_index(h, 8 if pair == 4 else 2 * pair + 1)
                                   + len(t_blocks(8 if pair == 4 else 2 * pair + 1)))
                        pe.wait_ge(p_free, u - 1)
                        nkt = 3 if pair == 4 else 2 * pair + 2
                        for kt in range(nkt):
                            lo, hi = (0, DEC) if pair == 4 else (P if kt == nkt - 1 else 0, 2 * P)
                            vt = 8 + kt if pair == 4 else kt
                            rows = DEC if vt == 10 else P
                            last = product(ps[:, 6 + u % 2, lo:hi], v_hi[b][0:rows, vt, :], v_lo[b][0:rows, vt, :],
                                           pt_hi[0:rows, kt, lo:hi], pt_lo[0:rows, kt, lo:hi],
                                           kt == 0, kt == nkt - 1)
                        last.then_inc(p_done, 1)

            def ret_projection(h, kind, g):
                b, key = h % 2, ("R", h, kind, g)
                u = p_order[key]
                bank = 6 + u % 2
                pe.wait_ge(p_free, u - 1)
                if kind in "QK":
                    n = ret_item(h, kind)
                    pe.wait_ge(w_low, n + 1)
                    c0, c1 = GROUPS[g]
                    for k in range(KT):
                        if h == 0 and kind == "Q" and g == 0:
                            pe.wait_ge(xn_in[k], 32)
                        last = product(ps[:, bank, 0:c1 - c0], w_hi[:, n % 2, k, :], w_lo[:, n % 2, k, :],
                                       xn_hi[:, k, c0:c1], xn_lo[:, k, c0:c1], k == 0, k == KT - 1)
                else:
                    n = ret_item(h, "V")
                    pe.wait_ge(w_low, n + 2)
                    c0, c1 = g * P, min(TOK, (g + 1) * P)
                    for k in range(KT):
                        out = ps[0:c1 - c0, bank, 0:DV].rearrange("p (s n) -> p s n", s=2)
                        last = product(out, xn_hi[:, k, c0:c1], xn_lo[:, k, c0:c1],
                                       w_hi[:, :, k, :], w_lo[:, :, k, :], k == 0, k == KT - 1)
                last.then_inc(p_done, 1)

            for kind, count in (("Q", NG), ("K", NG), ("V", 9)):
                for g in range(count):
                    ret_projection(0, kind, g)
            for h in range(RH):
                b = h % 2
                for s in retention_steps(h):
                    if s[0] == "F":
                        ret_projection(*s[1:])
                    elif s[0] == "C":
                        c = s[1]
                        n = 9 * h + c
                        c0, c1 = c * P, min(TOK, (c + 1) * P)
                        L = c1 - c0
                        if c == 0:
                            pe.wait_ge(rot_low, 1 + rot_index["R", h, "K", NG - 1])
                            pe.wait_ge(p_free, 1 + p_order["R", h, "V", 8])
                        if n:
                            pe.wait_ge(kd_low, n)
                        nc.tensor.transpose(ps[0:L, 3, 0:DK], rk_f[b][:, c0:c1], eye[:, :]).then_inc(kd_done, 1)
                        if n:
                            pe.wait_ge(sc_mid, n)
                        product(ps[0:L, 0, 0:L], rk_hi[b][:, c0:c1], rk_lo[b][:, c0:c1],
                                rq_hi[b][:, c0:c1], rq_lo[b][:, c0:c1]).then_inc(sc_done, 1)
                        pe.wait_ge(kd_low, n + 1)
                        if n:
                            pe.wait_ge(state_f, n)
                        product(ps[:, 4, 0:DV], kd_hi[0:L, :], kd_lo[0:L, :],
                                rv_hi[b][0:L, c, :], rv_lo[b][0:L, c, :]).then_inc(u_done, 1)
                        pe.wait_ge(sc_low, n + 1)
                        pe.wait_ge(state_low, 9 * h + c + 1)
                        if n:
                            pe.wait_ge(z_copy, n)
                        out = ps[0:L, 1, 0:DV]
                        product(out, rq_hi[b][:, c0:c1], rq_lo[b][:, c0:c1], s_hi[:, :], s_lo[:, :], True, False)
                        product(out, st_hi[0:L, 0:L], st_lo[0:L, 0:L],
                                rv_hi[b][0:L, c, :], rv_lo[b][0:L, c, :], False, True).then_inc(z_done, 1)
                    else:
                        c = s[1]
                        n = 9 * h + c
                        L = P if c < 8 else DEC
                        pe.wait_ge(z_norm, n + 1)
                        if n:
                            pe.wait_ge(zt_copy, n)
                        for j in range(2):
                            last = nc.tensor.transpose(ps[:, 2, j * P:j * P + L],
                                                       zn[n % 2][0:L, j * P:(j + 1) * P], eye[0:L, 0:L])
                        last.then_inc(zt_done, 1)

            pe.wait_ge(zt_copy, 9 * RH)
            pe.wait_ge(state_f, 9 * RH)
            with pe.Fori(0, 4) as i:
                for j in range(2):
                    item_units((I_GATE + j) % 2, 2 * i + (I_GATE + j), 3 * j,
                               (g_free, 6 * i + (F_GATE + 3 * j - 5)), xn_hi, xn_lo)
            pe.wait_ge(g_low, 24)
            for n0, free0, act0, branch in ((I_M1, F_M1, A_M1, 0), (I_M2, F_M2, A_M2, 1)):
                if branch:
                    for t in range(KT):
                        pe.wait_ge(ym_in[t], 32)
                with pe.Fori(0, 8) as i:
                    item_units(n0 % 2, 2 * i + n0, 0, (g_act, 3 * i + (act0 - 2)), xn_hi, xn_lo)
                    item_units((n0 + 1) % 2, 2 * i + (n0 + 1), 3, (g_free, 3 * i + (free0 - 2)), y_hi, y_lo)
            pe.wait_ge(split_lo, KT)
            with pe.Fori(0, 4) as i:
                for j in range(2):
                    item_units((I_OUT + j) % 2, 2 * i + (I_OUT + j), 3 * j,
                               (g_free, 6 * i + (F_OUT + 3 * j - 5)), xn_hi, xn_lo)

            pe.wait_ge(summed, SUM_OUT + 24)
            feature_sums(3, res_sq)
            pe.wait_ge(norm_low, 2 * KT + 6)
            n0, free0, act0, low0 = I_FFN, F_FFN, A_FFN, 24
            for _, tiles in FFN_GROUPS:
                pe.wait_ge(g_free, free0 - 3)
                with pe.Fori(0, tiles) as i:
                    item_units(n0 % 2, 2 * i + n0, 0, (g_act, 3 * i + (act0 - 2)), xn_hi, xn_lo)
                    item_units((n0 + 1) % 2, 2 * i + (n0 + 1), 3, (g_free, 3 * i + (free0 - 2)), xn_hi, xn_lo)
                n0, free0, act0, low0 = n0 + 2 * tiles, free0 + 3 * tiles, act0 + 3 * tiles, low0 + 3 * tiles
                pe.wait_ge(g_low, low0)
                with pe.Fori(0, 4) as i:
                    for j in range(2):
                        item_units((n0 + j) % 2, 2 * i + (n0 + j), 3 * j,
                                   (g_free, 6 * i + (free0 + 3 * j - 5)), y_hi, y_lo, blocks=tiles)
                n0, free0 = n0 + 8, free0 + 24
            pe.wait_ge(summed, SUM_FIN + 24)
            feature_sums(4, res_sq)

        @block.scalar
        def _(act):
            def split_high(slot, n, turn):
                act.wait_ge(stage_in[slot], 16 * turn + 16)
                nc.scalar.activation(w_hi[:, slot, :, :], stage[slot][:, :, :], ACT.Copy).then_inc(w_high, 1)

            def item(n):
                split_high(n % 2, n, n // 2)

            def in_loop(i, n1):
                split_high(n1 % 2, None, i + n1 // 2)

            def squares(first, src, tiles, square):
                for t in range(tiles):
                    k = first + t
                    if first == 0:
                        act.wait_ge(x_in[t], 16)
                    if k >= 2:
                        act.wait_ge(summed, k - 1)
                    nc.scalar.activation(square[:, k % 2, :], src[:, t, :], ACT.Square).then_inc(squared, 1)

            def roots(k, width):
                for g, (c0, c1) in enumerate(GROUPS):
                    act.wait_ge(stat_done, 3 * k + g + 1)
                    if k or g:
                        act.wait_ge(inv_done, 3 * k + g)
                    nc.scalar.activation(root[:, 0:c1 - c0], ps[:, 7, 0:c1 - c0], ACT.Sqrt,
                                         bias=eps[:, :], scale=1.0 / width).then_inc(root_done, 1)

            def highs(first, dst, src, tiles):
                for t in range(tiles):
                    act.wait_ge(scaled, first + t + 1)
                    nc.scalar.activation(dst[:, t, 0:TOK], src[:, t, :], ACT.Copy).then_inc(norm_high, 1)

            squares(0, xt, KT, square)
            act.wait_ge(set_up, 1)
            roots(0, D_MODEL)
            item(0)
            act.wait_ge(summed, KT)
            highs(0, xn_hi, xt, KT)
            for j in range(N_A):
                act.wait_ge(g_done, G_A + 3 * j + 1)
                item(I_A + j + 1)
            for g, (c0, c1) in enumerate(GROUPS):
                act.wait_ge(rot_sum, g + 1)
                nc.scalar.activation(kp_hi[0:ROPE, c0:c1], kpe_out[0:ROPE, c0:c1], ACT.Copy)
                nc.scalar.activation(kp_hi[ROPE:P, c0:c1], kpe_out[0:ROPE, c0:c1], ACT.Copy).then_inc(rot_high, 1)
            act.wait_ge(norm_low, KT)
            squares(KT, ckv_raw, 2, square_late)
            roots(1, KV_LORA)
            squares(KT + 2, cq_raw, 4, square_late)
            roots(2, Q_LORA)
            act.wait_ge(g_done, G_GATE)
            act.wait_ge(spill_out, 2 * KT * 16)
            highs(KT, ckn_hi, ckv_raw, 2)
            highs(KT + 2, cqn_hi, cq_raw, 4)
            act.wait_ge(cache_landed, 32)
            nc.scalar.activation(ckn_hi[:, :, TOK:KEYS], cache_in[:, :, :], ACT.Copy)
            nc.scalar.activation(kp_hi[0:ROPE, TOK:KEYS], cpe_in[0:ROPE, :], ACT.Copy)
            nc.scalar.activation(kp_hi[ROPE:P, TOK:KEYS], cpe_in[0:ROPE, :], ACT.Copy).then_inc(cache_high, 1)

            def projection(h, kind, g):
                b, key = h % 2, ("M", h, kind, g)
                u = p_order[key]
                if kind != "R":
                    act.wait_ge(p_done, u + 1)
                bank = 6 + u % 2
                if kind == "K":
                    c0, c1 = KEY_GROUPS[g]
                    nc.scalar.activation(k_hi[b][:, c0:c1], ps[:, bank, 0:c1 - c0], ACT.Copy).then_inc(p_high, 1)
                elif kind == "V":
                    full = 4 if g < 2 else 2
                    dst = v_hi[b][:, 4 * g:4 * g + full, :]
                    src = ps[:, bank, 0:full * P].rearrange("p (t e) -> p t e", t=full)
                    ins = nc.scalar.activation(dst, src, ACT.Copy)
                    if g == 2:
                        ins = nc.scalar.activation(v_hi[b][0:DEC, 10, :], ps[0:DEC, bank, 256:384], ACT.Copy)
                    ins.then_inc(p_high, 1)
                elif kind == "Q":
                    c0, c1 = GROUPS[g]
                    nc.scalar.activation(q_hi[b][:, c0:c1], ps[:, bank, 0:c1 - c0], ACT.Copy).then_inc(p_high, 1)
                else:
                    c0, c1 = GROUPS[g]
                    r = rot_index[key]
                    act.wait_ge(rot_sum, r + 1)
                    total = rot_total
                    if h:
                        act.wait_ge(s_done, 9 * h)
                    nc.scalar.activation(qr[0][0:64, c0:c1], total[0:64, 0:c1 - c0], ACT.Copy)
                    nc.scalar.activation(qr[1][64:128, c0:c1], total[64:128, 0:c1 - c0],
                                         ACT.Copy).then_inc(rot_high, 1)
                n = mla_item(h, kind)
                if g == 0 and kind in "KR":
                    if kind == "R":
                        act.wait_ge(p_done, u + 1)
                    item(n + 1)

            for kind in "KVQR":
                for g in range(NG):
                    projection(0, kind, g)
            for h in range(MH):
                b = h % 2
                for s in attention_steps(h):
                    if s[0] == "F":
                        projection(*s[1:])
                    elif s[0] == "S":
                        n = s_index(h, s[1])
                        _, nk, nq = keys_of(s[1])
                        act.wait_ge(max_done, n + 1)
                        if n >= 2:
                            act.wait_ge(t_done, t_end(n - 2))
                        bank = 2 * (n % 2)
                        src = ps[0:nq, bank:bank + 2, :].rearrange("p b k -> p (b k)")[:, 0:nk]
                        nc.scalar.activation(p_exp[n % 2][0:nq, 0:nk], src, ACT.Exp,
                                             bias=negmax[0:nq, n % 2, 0:1], scale=SCALE,
                                             accum_out=rowsum[0:nq, n % 2, 0:1]).then_inc(exp_done, 1)
                    elif s[0] == "T":
                        tile = s[1]
                        _, nk, nq = keys_of(tile)
                        q0 = P * (tile % 2) if tile < 8 else 0
                        if h == 0 and tile == 8:
                            act.wait_ge(kv_out, 32)
                        for i, (k0, nb) in enumerate(t_blocks(tile)):
                            t = t_index(h, tile) + i
                            act.wait_ge(t_done, t + 1)
                            if i == 0 and (tile % 2 == 0) and (h or tile != 8):
                                act.wait_ge(p_done, 1 + (p_order["M", h - 1, "O", 3] if tile == 8 else
                                                     p_order["M", h, "O", tile // 2 - 1 if tile else 4]))
                            full = nb if tile < 8 else 2
                            src = ps[:, 4 + t % 2, 0:full * P].rearrange("p (k q) -> p k q", k=full)[:, :, 0:nq]
                            ins = nc.scalar.activation(pt_hi[:, k0:k0 + full, q0:q0 + nq], src, ACT.Copy)
                            if tile == 8:
                                ins = nc.scalar.activation(pt_hi[0:DEC, 2, 0:nq],
                                                           ps[0:DEC, 4 + t % 2, 2 * P:2 * P + nq], ACT.Copy)
                            ins.then_inc(t_high, 1)
                    else:
                        n = o_index(h, s[1])
                        w = DEC if s[1] == 4 else 2 * P
                        u = p_order["M", h, "O", s[1]]
                        act.wait_ge(p_done, u + 1)
                        if n >= 2:
                            act.wait_ge(o_out[n % 2], 16 * (n // 2))
                        nc.scalar.activation(out_hl[n % 2][:, 0, 0:w], ps[:, 6 + u % 2, 0:w],
                                             ACT.Copy).then_inc(p_high, 1)

            def ret_projection(h, kind, g):
                b, key = h % 2, ("R", h, kind, g)
                u = p_order[key]
                n = ret_item(h, kind)
                if kind in "QK":
                    r = rot_index[key]
                    c0, c1 = GROUPS[g]
                    if g == 0:
                        act.wait_ge(p_done, u + 1)
                        item(n + 1)
                    act.wait_ge(rot_sum, r + 1)
                    src = rk_f[b][:, c0:c1] if kind == "K" else rot_total[:, 0:c1 - c0]
                    dst = rk_hi if kind == "K" else rq_hi
                    nc.scalar.activation(dst[b][:, c0:c1], src, ACT.Copy).then_inc(rot_high, 1)
                    if kind == "K" and g == NG - 1:
                        act.wait_ge(p_done, u + 1)
                        item(n + 2)
                else:
                    L = P if g < 8 else DEC
                    act.wait_ge(p_done, u + 1)
                    nc.scalar.activation(rv_hi[b][0:L, g, :], ps[0:L, 6 + u % 2, 0:DV],
                                         ACT.Copy).then_inc(p_high, 1)
                    if g == 8:
                        item(n + 2)

            for kind, count in (("Q", NG), ("K", NG), ("V", 9)):
                for g in range(count):
                    ret_projection(0, kind, g)
            for h in range(RH):
                for s in retention_steps(h):
                    if s[0] == "F":
                        ret_projection(*s[1:])
                    elif s[0] == "C":
                        c = s[1]
                        n = 9 * h + c
                        L = P if c < 8 else DEC
                        col = 1 if c < 8 else 2
                        if c == 0 or c == 8:
                            act.wait_ge(state_load, 2 * h + 1 + (c == 8))
                            if n:
                                act.wait_ge(z_done, n)
                            nc.scalar.activation(s_hi[:, :], s_f[:, :], ACT.Copy).then_inc(state_high, 1)
                        act.wait_ge(kd_done, n + 1)
                        if n:
                            act.wait_ge(u_done, n)
                        nc.scalar.activation(kd_hi[0:L, :], ps[0:L, 3, 0:DK], ACT.Copy,
                                             scale=dcol[0:L, h, col:col + 1]).then_inc(kd_high, 1)
                        act.wait_ge(sc_mid, n + 1)
                        if n:
                            act.wait_ge(z_done, n)
                        nc.scalar.activation(st_hi[0:L, 0:L], st_f[0:L, 0:L], ACT.Copy).then_inc(sc_high, 1)
                        act.wait_ge(z_done, n + 1)
                        if n:
                            act.wait_ge(z_norm, n)
                        nc.scalar.activation(zs[0:L, :], ps[0:L, 1, 0:DV], ACT.Copy,
                                             scale=dcol[0:L, h, 0:1]).then_inc(z_copy, 1)
                        if c < 7:
                            act.wait_ge(state_f, n + 1)
                            nc.scalar.activation(s_hi[:, :], s_f[:, :], ACT.Copy).then_inc(state_high, 1)
                    else:
                        c = s[1]
                        n = 9 * h + c
                        L = P if c < 8 else DEC
                        act.wait_ge(zt_done, n + 1)
                        if n >= 2:
                            act.wait_ge(zt_out[n % 2], 32 * (n // 2))
                        for j in range(2):
                            ins = nc.scalar.activation(zt[n % 2][:, j, 0:L], ps[:, 2, j * P:j * P + L], ACT.Copy,
                                                       scale=gains[:, G_GN + 2 * h + j:G_GN + 2 * h + j + 1])
                        ins.then_inc(zt_copy, 1)

            with act.Fori(0, 4) as i:
                for j in range(2):
                    for g, (c0, c1) in enumerate(GROUPS):
                        k = 3 * j + g
                        act.wait_ge(g_done, 6 * i + (G_GATE + k + 1))
                        act.wait_ge(g_free, 6 * i + (F_GATE + k))
                        nc.scalar.activation(tmp[3][:, 0:c1 - c0], ps[:, k, 0:c1 - c0],
                                             ACT.Silu).then_inc(g_act, 1)
                        if g == 0:
                            in_loop(i, I_GATE + 1 + j)
                        act.wait_ge(g_free, 6 * i + (F_GATE + k + 1))
                        nc.scalar.activation(y_hi[:, 2 * i + j, c0:c1], tmp[2][:, 0:c1 - c0],
                                             ACT.Copy).then_inc(g_high, 1)
            act.wait_ge(g_low, 24)
            for n0, u0, free0 in ((I_M1, G_M1, F_M1), (I_M2, G_M2, F_M2)):
                with act.Fori(0, 8) as i:
                    for g, (c0, c1) in enumerate(GROUPS):
                        act.wait_ge(g_done, 6 * i + (u0 + g + 1))
                        act.wait_ge(g_free, 3 * i + (free0 - 2 + g))
                        nc.scalar.activation(tmp[g][:, 0:c1 - c0], ps[:, g, 0:c1 - c0],
                                             ACT.Sigmoid).then_inc(g_act, 1)
                        if g == 0:
                            in_loop(i, n0 + 1)
                    act.wait_ge(g_done, 6 * i + (u0 + 4))
                    in_loop(i, n0 + 2)
            act.wait_ge(g_done, G_OUT)
            act.wait_ge(m_add, 24)
            for t in range(KT):
                nc.scalar.activation(xn_hi[:, t, :], res[:, t, :], ACT.Copy).then_inc(split_hi, 1)

            def residual_squares(i, j, g, c0, c1, free0, sum0):
                k = 3 * j + g
                act.wait_ge(g_free, 6 * i + (free0 + k + 1))
                act.wait_ge(summed, 6 * i + (sum0 + k - 1))
                nc.scalar.activation(tmp[4 + k % 2][:, 0:c1 - c0], res[:, 2 * i + j, c0:c1],
                                     ACT.Square).then_inc(squared, 1)

            with act.Fori(0, 4) as i:
                for j in range(2):
                    for g, (c0, c1) in enumerate(GROUPS):
                        if g == 0:
                            act.wait_ge(g_done, 6 * i + (G_OUT + 3 * j + 1))
                            in_loop(i, I_OUT + 1 + j)
                        residual_squares(i, j, g, c0, c1, F_OUT, SUM_OUT)
            roots(3, D_MODEL)
            for t in range(KT):
                act.wait_ge(scaled, KT + 6 + t + 1)
                nc.scalar.activation(xn_hi[:, t, :], norm_f[t % 2][:, :], ACT.Copy).then_inc(norm_high, 1)
            n0, u0, free0, sum0 = I_FFN, G_FFN, F_FFN, SUM_FIN
            for f, (_, tiles) in enumerate(FFN_GROUPS):
                with act.Fori(0, tiles) as i:
                    for g, (c0, c1) in enumerate(GROUPS):
                        act.wait_ge(g_done, 6 * i + (u0 + g + 1))
                        act.wait_ge(g_free, 3 * i + (free0 - 2 + g))
                        nc.scalar.activation(tmp[g][:, 0:c1 - c0], ps[:, g, 0:c1 - c0],
                                             ACT.Silu).then_inc(g_act, 1)
                        if g == 0:
                            in_loop(i, n0 + 1)
                    act.wait_ge(g_done, 6 * i + (u0 + 4))
                    in_loop(i, n0 + 2)
                    for g, (c0, c1) in enumerate(GROUPS):
                        act.wait_ge(g_free, 3 * i + (free0 + g + 1))
                        nc.scalar.activation(y_hi[:, i, c0:c1], tmp[3 + g % 2][:, 0:c1 - c0],
                                             ACT.Copy).then_inc(g_high, 1)
                n0, u0, free0 = n0 + 2 * tiles, u0 + 6 * tiles, free0 + 3 * tiles
                last_group = f == len(FFN_GROUPS) - 1

                def down(i, j, split):
                    for g, (c0, c1) in enumerate(GROUPS):
                        if g == 0 and split:
                            act.wait_ge(g_done, 6 * i + (u0 + 3 * j + 1))
                            in_loop(i, n0 + 1 + j)
                        if last_group:
                            residual_squares(i, j, g, c0, c1, free0, sum0)

                with act.Fori(0, 3 if last_group else 4) as i:
                    for j in range(2):
                        down(i, j, True)
                if last_group:
                    down(3, 0, True)
                    down(3, 1, False)
                n0, u0, free0 = n0 + 8, u0 + 24, free0 + 24
            roots(4, D_MODEL)

        @block.vector
        def _(dve):
            chained = [0]

            def chain(ins):
                chained[0] += 1
                ins.then_inc(v_chain, 1)
                dve.wait_ge(v_chain, chained[0])

            def split_low(slot, n):
                dve.wait_ge(w_high, n + 1)
                nc.vector.tensor_tensor(w_lo[:, slot, :, :], stage[slot][:, :, :],
                                        w_hi[:, slot, :, :].bitcast(F32), ALU.subtract).then_inc(w_low, 1)

            def item(n):
                split_low(n % 2, n)

            def in_loop(i, n):
                split_low(n % 2, 2 * i + n)

            def low(dst, full, high):
                return nc.vector.tensor_tensor(dst, full, high.bitcast(F32), ALU.subtract)

            def sums(first, tiles, square):
                for t in range(tiles):
                    k = first + t
                    dve.wait_ge(squared, k + 1)
                    if t:
                        dve.wait_ge(summed, k)
                        ins = nc.vector.tensor_tensor(sumsq[:, :], sumsq[:, :], square[:, k % 2, :], ALU.add)
                    else:
                        ins = nc.vector.tensor_copy(sumsq[:, :], square[:, k % 2, :])
                    ins.then_inc(summed, 1)

            def inverses(k, dst):
                for g, (c0, c1) in enumerate(GROUPS):
                    dve.wait_ge(root_done, 3 * k + g + 1)
                    nc.vector.reciprocal(dst[:, c0:c1], root[:, 0:c1 - c0]).then_inc(inv_done, 1)
                dve.wait_ge(inv_done, 3 * k + 3)

            def normalise(src, dst, gain, inverse):
                nc.vector.scalar_tensor_tensor(dst, src, gains[:, gain:gain + 1], inverse[:, :],
                                               ALU.mult, ALU.mult).then_inc(scaled, 1)

            def swap_products(out, bank, width, rows, sin, c0, c1):
                half_rows = rows[1]
                for r in range(0, rows[0], 2 * half_rows):
                    for x, y in ((r, r + half_rows), (r + half_rows, r)):
                        last = nc.vector.tensor_tensor(out[x:x + half_rows, 0:width],
                                                       ps[y:y + half_rows, bank, 0:width],
                                                       sin[y:y + half_rows, c0:c1], ALU.mult)
                return last

            def rotate(r, bank, rows, half_rows, cos, sin, c0, c1, freed):
                if r:
                    dve.wait_ge(rot_sum, r)
                nc.vector.tensor_tensor(rot_cos[0:rows, 0:c1 - c0], ps[0:rows, bank, 0:c1 - c0],
                                        cos[0:rows, c0:c1], ALU.mult)
                swap_products(rot_sin, bank, c1 - c0, (rows, half_rows), sin, c0, c1).then_inc(freed, 1)

            nc.vector.memset(ones[:, :], 1.0)
            nc.vector.memset(half[:, :], -0.5)
            nc.vector.memset(eps[:, :], EPS).then_inc(set_up, 1)
            sums(0, KT, square)
            inverses(0, inv)
            dve.wait_ge(consts_in, 32)
            for t in range(KT):
                normalise(xt[:, t, :], xt[:, t, :], G_MIX + t, inv)
                if t == 0:
                    item(0)
            for j in range(N_A):
                bank = 3 * (j % 2)
                for g, (c0, c1) in enumerate(GROUPS):
                    dve.wait_ge(g_done, G_A + 3 * j + g + 1)
                    if j < N_A - 1:
                        dst = ckv_raw[:, j, c0:c1] if j < 2 else cq_raw[:, j - 2, c0:c1]
                        nc.vector.tensor_copy(dst, ps[:, bank + g, 0:c1 - c0]).then_inc(g_free, 1)
                    else:
                        if g == 0:
                            dve.wait_ge(tables_in, 32)
                        rotate(g, bank + g, ROPE, ROPE // 2, cos64, sin64, c0, c1, g_free)
                    if g == 0:
                        item(I_A + j + 1)
            for g, (c0, c1) in enumerate(GROUPS):
                dve.wait_ge(rot_high, g + 1)
                low(kp_lo[0:ROPE, c0:c1], kpe_out[0:ROPE, c0:c1], kp_hi[0:ROPE, c0:c1])
                low(kp_lo[ROPE:P, c0:c1], kpe_out[0:ROPE, c0:c1], kp_hi[0:ROPE, c0:c1]).then_inc(rot_low, 1)
            dve.wait_ge(stat_done, 3)
            sums(KT, 2, square_late)
            inverses(1, inv)
            for t in range(2):
                normalise(ckv_raw[:, t, :], ckv_raw[:, t, :], G_KV + t, inv)
            dve.wait_ge(stat_done, 6)
            sums(KT + 2, 4, square_late)
            dve.wait_ge(scaled, KT + 2)
            inverses(2, inv)
            for t in range(4):
                normalise(cq_raw[:, t, :], cq_raw[:, t, :], G_Q + t, inv)
            dve.wait_ge(cache_high, 1)
            low(ckn_lo[:, :, TOK:KEYS], cache_in[:, :, :], ckn_hi[:, :, TOK:KEYS])
            low(kp_lo[0:ROPE, TOK:KEYS], cpe_in[0:ROPE, :], kp_hi[0:ROPE, TOK:KEYS])
            low(kp_lo[ROPE:P, TOK:KEYS], cpe_in[0:ROPE, :], kp_hi[0:ROPE, TOK:KEYS]).then_inc(cache_low, 1)

            def projection(h, kind, g):
                b, key = h % 2, ("M", h, kind, g)
                u = p_order[key]
                bank = 6 + u % 2
                n = mla_item(h, kind)
                if kind == "R":
                    r = rot_index[key]
                    c0, c1 = GROUPS[g]
                    dve.wait_ge(p_done, u + 1)
                    rotate(r, bank, P, ROPE // 2, cos64, sin64, c0, c1, p_free)
                    if g == 0:
                        item(n + 1)
                    dve.wait_ge(rot_high, r + 1)
                    w = c1 - c0
                    low(qr[0][64:128, c0:c1], rot_total[0:64, 0:w], qr[0][0:64, c0:c1])
                    low(qr[1][0:64, c0:c1], rot_total[64:128, 0:w], qr[1][64:128, c0:c1]).then_inc(rot_low, 1)
                    return
                dve.wait_ge(p_high, u + 1 - sum(1 for k in rotated if p_order[k] < u))
                if kind == "K":
                    c0, c1 = KEY_GROUPS[g]
                    low(k_lo[b][:, c0:c1], ps[:, bank, 0:c1 - c0], k_hi[b][:, c0:c1]).then_inc(p_free, 1)
                    if g == 0:
                        item(n + 1)
                elif kind == "V":
                    full = 4 if g < 2 else 2
                    ins = low(v_lo[b][:, 4 * g:4 * g + full, :],
                              ps[:, bank, 0:full * P].rearrange("p (t e) -> p t e", t=full),
                              v_hi[b][:, 4 * g:4 * g + full, :])
                    if g == 2:
                        ins = low(v_lo[b][0:DEC, 10, :], ps[0:DEC, bank, 256:384], v_hi[b][0:DEC, 10, :])
                    ins.then_inc(p_free, 1)
                else:
                    c0, c1 = GROUPS[g]
                    low(q_lo[b][:, c0:c1], ps[:, bank, 0:c1 - c0], q_hi[b][:, c0:c1]).then_inc(p_free, 1)

            for kind in "KVQR":
                for g in range(NG):
                    projection(0, kind, g)
            for h in range(MH):
                for s in attention_steps(h):
                    if s[0] == "F":
                        projection(*s[1:])
                    elif s[0] == "S":
                        n = s_index(h, s[1])
                        _, nk, nq = keys_of(s[1])
                        bank = 2 * (n % 2)
                        scores = ps[0:nq, bank:bank + 2, :].rearrange("p b k -> p (b k)")
                        dve.wait_ge(s_done, n + 1)
                        if s[1] < 8:
                            chain(nc.vector.memset(scores[0:64, nk - 64:nk], NEG))
                        chain(nc.vector.reduce_max(negmax[0:nq, n % 2, 1:2], scores[:, 0:nk], AX.X))
                        nc.vector.tensor_scalar(negmax[0:nq, n % 2, 0:1], negmax[0:nq, n % 2, 1:2],
                                                -SCALE, None, ALU.mult).then_inc(max_done, 1)
                    elif s[0] == "T":
                        tile = s[1]
                        n = s_index(h, tile)
                        _, nk, nq = keys_of(tile)
                        q0 = P * (tile % 2) if tile < 8 else 0
                        dve.wait_ge(exp_done, n + 1)
                        chain(nc.vector.reciprocal(rowsum[0:nq, n % 2, 1:2], rowsum[0:nq, n % 2, 0:1]))
                        nc.vector.tensor_scalar(p_exp[n % 2][0:nq, 0:nk], p_exp[n % 2][0:nq, 0:nk],
                                                rowsum[0:nq, n % 2, 1:2], None, ALU.mult).then_inc(prob_done, 1)
                        for i, (k0, nb) in enumerate(t_blocks(tile)):
                            t = t_index(h, tile) + i
                            dve.wait_ge(t_high, t + 1)
                            full = nb if tile < 8 else 2
                            src = ps[:, 4 + t % 2, 0:full * P].rearrange("p (k q) -> p k q", k=full)[:, :, 0:nq]
                            ins = low(pt_lo[:, k0:k0 + full, q0:q0 + nq], src, pt_hi[:, k0:k0 + full, q0:q0 + nq])
                            if tile == 8:
                                ins = low(pt_lo[0:DEC, 2, 0:nq], ps[0:DEC, 4 + t % 2, 2 * P:2 * P + nq],
                                          pt_hi[0:DEC, 2, 0:nq])
                            ins.then_inc(t_low, 1)
                    else:
                        n = o_index(h, s[1])
                        w = DEC if s[1] == 4 else 2 * P
                        u = p_order["M", h, "O", s[1]]
                        dve.wait_ge(p_high, u + 1 - sum(1 for k in rotated if p_order[k] < u))
                        low(out_hl[n % 2][:, 1, 0:w], ps[:, 6 + u % 2, 0:w],
                            out_hl[n % 2][:, 0, 0:w]).then_inc(p_free, 1)

            def ret_projection(h, kind, g):
                b, key = h % 2, ("R", h, kind, g)
                u = p_order[key]
                bank = 6 + u % 2
                n = ret_item(h, kind)
                if kind in "QK":
                    r = rot_index[key]
                    c0, c1 = GROUPS[g]
                    dve.wait_ge(p_done, u + 1)
                    rotate(r, bank, P, DK // 2, cos128, sin128, c0, c1, p_free)
                    if g == 0:
                        item(n + 1)
                    if kind == "K" and g == NG - 1:
                        item(n + 2)
                else:
                    L = P if g < 8 else DEC
                    dve.wait_ge(p_high, u + 1 - sum(1 for k in rotated if p_order[k] < u))
                    low(rv_lo[b][0:L, g, :], ps[0:L, bank, 0:DV], rv_hi[b][0:L, g, :]).then_inc(p_free, 1)
                    if g == 8:
                        item(n + 2)

            def state_low_part():
                low(s_lo[:, :], s_f[:, :], s_hi[:, :]).then_inc(state_low, 1)

            dve.wait_ge(tables_in, 32 + 64)
            for kind, count in (("Q", NG), ("K", NG), ("V", 9)):
                for g in range(count):
                    ret_projection(0, kind, g)
            for h in range(RH):
                gamma = 1.0 - 2.0 ** (-5.0 - h)
                for s in retention_steps(h):
                    if s[0] == "F":
                        ret_projection(*s[1:])
                    elif s[0] == "C":
                        c = s[1]
                        n = 9 * h + c
                        L = P if c < 8 else DEC
                        col = 1 if c < 8 else 2
                        if c == 0:
                            if h:
                                dve.wait_ge(state_out, 16 * 2 * h)
                            nc.vector.memset(s_f[:, :], 0.0).then_inc(state_load, 1)
                        if c == 8:
                            dve.wait_ge(state_out, 16 * (2 * h + 1))
                            dve.wait_ge(state_in, 16 * (h + 1))
                            nc.vector.tensor_copy(s_f[:, :], s_in[:, :]).then_inc(state_load, 1)
                        if c in (0, 8):
                            dve.wait_ge(state_high, 9 * h + c + 1)
                            state_low_part()
                        dve.wait_ge(kd_high, n + 1)
                        nc.vector.scalar_tensor_tensor(kd_lo[0:L, :], ps[0:L, 3, 0:DK],
                                                       dcol[0:L, h, col:col + 1], kd_hi[0:L, :].bitcast(F32),
                                                       ALU.mult, ALU.subtract).then_inc(kd_low, 1)
                        dve.wait_ge(sc_done, n + 1)
                        nc.vector.tensor_tensor(st_f[0:L, 0:L], ps[0:L, 0, 0:L], dmask[0:L, h, 0:L],
                                                ALU.mult).then_inc(sc_mid, 1)
                        dve.wait_ge(sc_high, n + 1)
                        low(st_lo[0:L, 0:L], st_f[0:L, 0:L], st_hi[0:L, 0:L]).then_inc(sc_low, 1)
                        dve.wait_ge(u_done, n + 1)
                        dve.wait_ge(state_high, 9 * h + c + 1)
                        nc.vector.scalar_tensor_tensor(s_f[:, :], s_f[:, :], gamma ** L, ps[:, 4, 0:DV],
                                                       ALU.mult, ALU.add).then_inc(state_f, 1)
                        if c < 7:
                            dve.wait_ge(state_high, 9 * h + c + 2)
                            state_low_part()
                    else:
                        c = s[1]
                        n = 9 * h + c
                        L = P if c < 8 else DEC
                        dve.wait_ge(z_copy, n + 1)
                        chain(nc.vector.bn_stats(bnst[0:L, n % 2, :], zs[0:L, :]))
                        nc.vector.bn_aggr(mv[0:L, n % 2, :], bnst[0:L, n % 2, :]).then_inc(z_stat, 1)
                        dve.wait_ge(z_rstd, n + 1)
                        if n >= 2:
                            dve.wait_ge(zt_done, n - 1)
                        nc.vector.tensor_scalar(zn[n % 2][0:L, :], zs[0:L, :], mv[0:L, n % 2, 0:1],
                                                rstd[0:L, n % 2, :], ALU.subtract, ALU.mult).then_inc(z_norm, 1)

            with dve.Fori(0, 4) as i:
                for j in range(2):
                    for g, (c0, c1) in enumerate(GROUPS):
                        k = 3 * j + g
                        w = c1 - c0
                        dve.wait_ge(g_act, 6 * i + (k + 1))
                        dve.wait_ge(yr_in[k % 2], 48 * i + 16 * (k // 2 + 1))
                        nc.vector.tensor_tensor(tmp[2][:, 0:w], tmp[3][:, 0:w], tmp[k % 2][:, 0:w],
                                                ALU.mult).then_inc(g_free, 1)
                        if g == 0:
                            in_loop(i, I_GATE + 1 + j)
                        dve.wait_ge(g_high, 6 * i + (k + 1))
                        low(y_lo[:, 2 * i + j, c0:c1], tmp[2][:, 0:w], y_hi[:, 2 * i + j, c0:c1]).then_inc(g_low, 1)
                        dve.wait_ge(g_low, 6 * i + (k + 1))
            dve.wait_ge(state_out, 16 * 2 * RH)
            for n0, u0, act0, free0 in ((I_M1, G_M1, A_M1, F_M1), (I_M2, G_M2, A_M2, F_M2)):
                with dve.Fori(0, 8) as i:
                    in_loop(i, n0 + 1)
                    for g, (c0, c1) in enumerate(GROUPS):
                        w = c1 - c0
                        dve.wait_ge(g_act, 3 * i + (act0 + g + 1))
                        dve.wait_ge(g_done, 6 * i + (u0 + 3 + g + 1))
                        dst = tmp[3 + g][:, 0:w] if n0 == I_M2 else res[:, i, c0:c1]
                        nc.vector.tensor_tensor(dst, ps[:, 3 + g, 0:w], tmp[g][:, 0:w], ALU.mult)\
                          .then_inc(g_free, 1)
                        if g == 0:
                            in_loop(i, n0 + 2)
                        if n0 == I_M2:
                            dve.wait_ge(g_free, 3 * i + (free0 + g + 1))
                            nc.vector.tensor_tensor(res[:, i, c0:c1], res[:, i, c0:c1], tmp[3 + g][:, 0:w],
                                                    ALU.add).then_inc(m_add, 1)
                    if n0 == I_M2:
                        dve.wait_ge(m_add, 3 * i + 3)
            for t in range(KT):
                dve.wait_ge(split_hi, t + 1)
                low(xn_lo[:, t, :], res[:, t, :], xn_hi[:, t, :]).then_inc(split_lo, 1)
            dve.wait_ge(split_lo, KT)
            nc.vector.memset(res_sq[:, :], 0.0).then_inc(set_up, 1)
            dve.wait_ge(set_up, 2)

            def residual_sum(i, j, g, c0, c1, sum0):
                k = 3 * j + g
                dve.wait_ge(squared, 6 * i + (sum0 + k + 1))
                dve.wait_ge(summed, 6 * i + (sum0 + k - 2))
                nc.vector.tensor_tensor(res_sq[:, c0:c1], res_sq[:, c0:c1], tmp[4 + k % 2][:, 0:c1 - c0],
                                        ALU.add).then_inc(summed, 1)

            with dve.Fori(0, 4) as i:
                for j in range(2):
                    for g, (c0, c1) in enumerate(GROUPS):
                        k = 3 * j + g
                        w = c1 - c0
                        dve.wait_ge(g_done, 6 * i + (G_OUT + k + 1))
                        dve.wait_ge(xres_in[k % 2], 48 * i + 16 * (k // 2 + 1))
                        nc.vector.tensor_tensor(res[:, 2 * i + j, c0:c1], ps[:, k, 0:w], tmp[k % 2][:, 0:w],
                                                ALU.add).then_inc(g_free, 1)
                        if g == 0:
                            in_loop(i, I_OUT + 1 + j)
                        residual_sum(i, j, g, c0, c1, SUM_OUT)
            inverses(3, res_inv)
            for t in range(KT):
                if t >= 2:
                    dve.wait_ge(norm_low, KT + 6 + t - 1)
                normalise(res[:, t, :], norm_f[t % 2][:, :], G_F + t, res_inv)
            dve.wait_ge(stat_done, 12)
            n0, u0, act0, free0, low0 = I_FFN, G_FFN, A_FFN, F_FFN, 24
            for f, (_, tiles) in enumerate(FFN_GROUPS):
                with dve.Fori(0, tiles) as i:
                    in_loop(i, n0 + 1)
                    for g, (c0, c1) in enumerate(GROUPS):
                        w = c1 - c0
                        dve.wait_ge(g_act, 3 * i + (act0 + g + 1))
                        dve.wait_ge(g_done, 6 * i + (u0 + 3 + g + 1))
                        if g == 2:
                            dve.wait_ge(g_low, 3 * i + (low0 + 1))
                        nc.vector.tensor_tensor(tmp[3 + g % 2][:, 0:w], ps[:, 3 + g, 0:w], tmp[g][:, 0:w],
                                                ALU.mult).then_inc(g_free, 1)
                        if g == 0:
                            in_loop(i, n0 + 2)
                        dve.wait_ge(g_high, 3 * i + (low0 + g + 1))
                        low(y_lo[:, i, c0:c1], tmp[3 + g % 2][:, 0:w], y_hi[:, i, c0:c1]).then_inc(g_low, 1)
                    dve.wait_ge(g_low, 3 * i + (low0 + 3))
                n0, u0 = n0 + 2 * tiles, u0 + 6 * tiles
                act0, free0, low0 = act0 + 3 * tiles, free0 + 3 * tiles, low0 + 3 * tiles
                last_group = f == len(FFN_GROUPS) - 1
                if last_group:
                    nc.vector.memset(res_sq[:, :], 0.0).then_inc(set_up, 1)
                    dve.wait_ge(set_up, 3)

                def down(i, j, split):
                    for g, (c0, c1) in enumerate(GROUPS):
                        k = 3 * j + g
                        dve.wait_ge(g_done, 6 * i + (u0 + k + 1))
                        nc.vector.tensor_tensor(res[:, 2 * i + j, c0:c1], res[:, 2 * i + j, c0:c1],
                                                ps[:, k, 0:c1 - c0], ALU.add).then_inc(g_free, 1)
                        if g == 0 and split:
                            in_loop(i, n0 + 1 + j)
                        if last_group:
                            residual_sum(i, j, g, c0, c1, SUM_FIN)

                with dve.Fori(0, 3 if last_group else 4) as i:
                    for j in range(2):
                        down(i, j, True)
                if last_group:
                    down(3, 0, True)
                    down(3, 1, False)
                n0, u0, free0 = n0 + 8, u0 + 24, free0 + 24
            inverses(4, res_inv)
            for t in range(KT):
                normalise(res[:, t, :], res[:, t, :], G_FIN + t, res_inv)

        @block.gpsimd
        def _(pool):
            def lows(first, dst, src, high, tiles):
                for t in range(tiles):
                    pool.wait_ge(norm_high, first + t + 1)
                    nc.gpsimd.tensor_tensor(dst(t), src(t), high(t).bitcast(F32), ALU.subtract)\
                      .then_inc(norm_low, 1)

            def add_products(r, dst, rows, width, freed, count):
                pool.wait_ge(freed, count)
                if r:
                    pool.wait_ge(rot_low, r) if r > NG else None
                nc.gpsimd.tensor_tensor(dst, rot_cos[0:rows, 0:width], rot_sin[0:rows, 0:width],
                                        ALU.add).then_inc(rot_sum, 1)

            lows(0, lambda t: xn_lo[:, t, :], lambda t: xt[:, t, :], lambda t: xn_hi[:, t, :], KT)
            for g, (c0, c1) in enumerate(GROUPS):
                add_products(g, kpe_out[0:ROPE, c0:c1], ROPE, c1 - c0, g_free, 3 * (N_A - 1) + g + 1)
            lows(KT, lambda t: ckn_lo[:, t, 0:TOK], lambda t: ckv_raw[:, t, :], lambda t: ckn_hi[:, t, 0:TOK], 2)
            lows(KT + 2, lambda t: cqn_lo[:, t, :], lambda t: cq_raw[:, t, :], lambda t: cqn_hi[:, t, :], 4)

            def rotary(h, kind, g):
                if kind == "R":
                    c0, c1 = GROUPS[g]
                    add_products(rot_index["M", h, "R", g], rot_total[:, 0:c1 - c0], P, c1 - c0,
                                 p_free, p_order["M", h, "R", g] + 1)

            for g in range(NG):
                rotary(0, "R", g)
            for h in range(MH):
                for s in attention_steps(h):
                    if s[0] == "F":
                        rotary(*s[1:])

            def ret_rotary(h, kind, g):
                if kind == "V":
                    return
                b, key = h % 2, ("R", h, kind, g)
                r = rot_index[key]
                c0, c1 = GROUPS[g]
                total = rk_f[b][:, c0:c1] if kind == "K" else rot_total[:, 0:c1 - c0]
                hi, lo = (rk_hi, rk_lo) if kind == "K" else (rq_hi, rq_lo)
                add_products(r, total, P, c1 - c0, p_free, p_order[key] + 1)
                pool.wait_ge(rot_high, r + 1)
                nc.gpsimd.tensor_tensor(lo[b][:, c0:c1], total, hi[b][:, c0:c1].bitcast(F32),
                                        ALU.subtract).then_inc(rot_low, 1)

            for kind in "QK":
                for g in range(NG):
                    ret_rotary(0, kind, g)
            for h in range(RH):
                for s in retention_steps(h):
                    if s[0] == "F":
                        ret_rotary(*s[1:])
                    elif s[0] == "Z":
                        n = 9 * h + s[1]
                        L = P if s[1] < 8 else DEC
                        pool.wait_ge(z_stat, n + 1)
                        nc.gpsimd.tensor_scalar(veps[0:L, n % 2, :], mv[0:L, n % 2, 1:2], EPS, None, ALU.add)\
                          .then_inc(pool_chain, 1)
                        pool.wait_ge(pool_chain, n + 1)
                        nc.gpsimd.tensor_tensor(rstd[0:L, n % 2, :], veps[0:L, n % 2, :], half[0:L, :],
                                                ALU.pow).then_inc(z_rstd, 1)
            lows(KT + 6, lambda t: xn_lo[:, t, :], lambda t: norm_f[t % 2][:, :], lambda t: xn_hi[:, t, :], KT)


def kernel(**inputs):
    import numpy as np
    import concourse.bacc as bacc
    from concourse.bass_utils import run_bass_kernel_spmd

    f32 = np.float32

    def feature_major(x):
        return np.ascontiguousarray(x.T.reshape(-1, P, x.shape[0]).transpose(1, 0, 2))

    def blocks(w, rows, cols):
        return w[:rows * P][:, cols].reshape(rows, P, -1).transpose(1, 0, 2)

    w_in = np.asarray(inputs["w_in"][0])
    w_uq, w_ukv = np.asarray(inputs["w_uq"][0]), np.asarray(inputs["w_ukv"][0])
    w_gu, w_down = np.asarray(inputs["w_gate_up"][0]), np.asarray(inputs["w_down"][0])
    offs = np.cumsum([0, RH * DK, RH * DK, RH * DV, RH * DV, Q_LORA, KV_LORA, ROPE, D_MODEL, D_MODEL])
    o_rq, o_rk, o_rv, o_rg, o_cq, o_ckv, o_kpe, o_ga, o_gb = offs[:9].tolist()

    W = np.zeros((N_ITEMS, P, 8, P), f32)
    n = [0]

    def put(*parts):
        k = 0
        for part in parts:
            W[n[0], :, k:k + part.shape[1], 0:part.shape[2]] = part
            k += part.shape[1]
        n[0] += 1

    def col(start, width=P):
        return slice(start, start + width)

    for start in [o_ckv, o_ckv + P] + [o_cq + P * t for t in range(4)]:
        put(blocks(w_in, KT, col(start)))
    put(blocks(w_in, KT, col(o_kpe, ROPE)))
    hq = NOPE + ROPE
    for h in range(MH):
        put(blocks(w_ukv, 2, col(h * (NOPE + VD))), blocks(w_ukv, 2, col(h * (NOPE + VD) + NOPE)),
            blocks(w_uq, 4, col(h * hq)))
        if h % 2 == 0:
            put(blocks(w_uq, 4, np.r_[h * hq + NOPE:(h + 1) * hq, (h + 1) * hq + NOPE:(h + 2) * hq]))
    for h in range(RH):
        put(blocks(w_in, KT, col(o_rq + P * h)))
        put(blocks(w_in, KT, col(o_rk + P * h)))
        halves = [col(o_rv + DV * h), col(o_rv + DV * h + P)]
        for half in (halves if n[0] % 2 == 0 else halves[::-1]):
            put(blocks(w_in, KT, half))
    for t in range(8):
        put(blocks(w_in, KT, col(o_rg + P * t)))
    for gate, w in ((o_ga, inputs["w_ret_o"][0]), (o_gb, inputs["w_mla_o"][0])):
        w = np.asarray(w)
        for t in range(KT):
            put(blocks(w_in, KT, col(gate + P * t)))
            put(blocks(w, KT, col(P * t)))
    for t in range(KT):
        put(blocks(np.asarray(inputs["w_out"][0]), KT, col(P * t)))
    for first, tiles in FFN_GROUPS:
        for t in range(first, first + tiles):
            put(blocks(w_gu, KT, col(P * t)))
            put(blocks(w_gu, KT, col(D_FF + P * t)))
        for t in range(KT):
            put(blocks(w_down[first * P:], tiles, col(P * t)))
    assert n[0] == N_ITEMS

    pos = np.concatenate([np.arange(SEQ), PAST + np.arange(DEC)]).astype(f32)

    def rotation(d):
        inv = (f32(10000.0) ** (-np.arange(0, d, 2, dtype=f32) / f32(d))).astype(f32)
        ang = pos[None, :] * inv[:, None]
        cos, sin = np.cos(ang), np.sin(ang)
        reps = P // d
        return (np.tile(np.concatenate([cos, cos]), (reps, 1)).astype(f32),
                np.tile(np.concatenate([sin, -sin]), (reps, 1)).astype(f32))

    cos64, sin64 = rotation(ROPE)
    cos128, sin128 = rotation(DK)
    row = np.arange(P, dtype=np.float64)
    dmask = np.zeros((P, RH, P), f32)
    dcol = np.zeros((P, RH, 3), f32)
    for h in range(RH):
        gamma = 1.0 - 2.0 ** (-5.0 - h)
        dmask[:, h, :] = np.where(row[None, :] >= row[:, None], gamma ** -(row[:, None] + 1), 0.0) * DK ** -0.5
        dcol[:, h, 0] = gamma ** (row + 1)
        dcol[:, h, 1] = gamma ** (P - 1 - row) * DK ** -0.5
        dcol[:DEC, h, 2] = gamma ** (DEC - 1 - row[:DEC]) * DK ** -0.5

    def gain(name):
        return np.asarray(inputs[name]).reshape(-1, P).T

    arrays = {
        "weights": W,
        "x": feature_major(np.concatenate([inputs["x_prompt"][0], inputs["x_sample"][0]])),
        "cache_ckv": feature_major(np.asarray(inputs["cache_ckv"][0, 0])),
        "cache_kpe": np.ascontiguousarray(np.asarray(inputs["cache_kpe"][0, 0]).T),
        "state": np.ascontiguousarray(np.asarray(inputs["state_ret"][0, 0]).transpose(1, 0, 2)),
        "gains": np.ascontiguousarray(np.concatenate(
            [gain(k) for k in ("norm_mix_w", "q_norm_w", "kv_norm_w", "ret_gn_w", "norm_ffn_w", "norm_final_w")],
            axis=1)),
        "eye": np.eye(P, dtype=f32),
        "cos64": cos64, "sin64": sin64, "cos128": cos128, "sin128": sin128, "dmask": dmask, "dcol": dcol,
    }
    nc = bacc.Bacc("TRN2", target_bir_lowering=False, num_devices=1)
    ins = {k: nc.dram_tensor(f"in_{k}", v.shape, F32, kind="ExternalInput").ap() for k, v in arrays.items()}
    shapes = {"y": (P, KT, TOK), "ckv": (P, 2, TOK), "kpe": (ROPE, TOK),
              "state_p": (P, RH, DV), "state_s": (P, RH, DV)}
    outs = {k: nc.dram_tensor(f"out_{k}", v, F32, kind="ExternalOutput").ap() for k, v in shapes.items()}
    build(nc, ins, outs)
    run = run_bass_kernel_spmd(nc, [{f"in_{k}": v for k, v in arrays.items()}], core_ids=[0])
    got = {k: run.results[0][f"out_{k}"] for k in shapes}

    def token_major(x):
        return np.ascontiguousarray(x.transpose(2, 1, 0).reshape(x.shape[2], -1))

    y, ckv = token_major(got["y"]), token_major(got["ckv"])
    kpe = np.ascontiguousarray(got["kpe"].T)
    state = [np.ascontiguousarray(got[k].transpose(1, 0, 2))[None, None] for k in ("state_p", "state_s")]
    return (y[None, :SEQ], y[None, SEQ:], ckv[None, None, :SEQ], kpe[None, None, :SEQ], state[0],
            ckv[None, None, SEQ:], kpe[None, None, SEQ:], state[1])
```

```python
from contextlib import ExitStack

import concourse.bass as bass
from concourse import mybir

F32 = mybir.dt.float32
F32R = mybir.dt.float32r
ALU = mybir.AluOpType
ACT = mybir.ActivationFunctionType
AX = mybir.AxisListType

P = 128
D_MODEL = 1024
SEQ = 1024
DEC = 64
PAST = 256
TOK = SEQ + DEC
KEYS = TOK + PAST
RH, DK, DV = 4, 128, 256
MH = 8
Q_LORA, KV_LORA, NOPE, ROPE, VD = 512, 256, 128, 64, 128
D_FF = ((8 * D_MODEL // 3 + 255) // 256) * 256
EPS = 1e-6
KT = D_MODEL // P
GROUPS = ((0, 384), (384, 768), (768, 1088))
KEY_GROUPS = ((0, 448), (448, 896), (896, 1344))
NG = 3
WIDE = 384
FT = D_FF // P
FFN_GROUPS = ((0, 8), (8, 8), (16, 6))
U = TOK * 4
SCALE = float(NOPE + ROPE) ** -0.5
NEG = -3.0e38

N_A = 7
N_MLA = 12
N_RET = 4 * RH
I_A = 0
I_MLA = I_A + N_A
I_RET = I_MLA + N_MLA
I_GATE = I_RET + N_RET
I_M1 = I_GATE + 8
I_M2 = I_M1 + 16
I_OUT = I_M2 + 16
I_FFN = I_OUT + 8
N_ITEMS = I_FFN + sum(2 * n + 8 for _, n in FFN_GROUPS)

G_A = 0
G_GATE = G_A + 3 * N_A
G_M1 = G_GATE + 3 * 8
G_M2 = G_M1 + 3 * 16
G_OUT = G_M2 + 3 * 16
G_FFN = G_OUT + 3 * 8


def attention_steps(head):
    order = [(h, tile) for h in (head, head + 1) if h < MH for tile in (8, 0, 1, 2, 3, 4, 5, 6, 7)]
    if head + 1 == MH:
        fill = [("R", 0, *unit) for unit in RET_UNITS]
        counts = (0, 0, 0, 1, 2, 3, 3, 3, 3)
    elif head % 2:
        fill = [("M", head + 1, kind, g) for kind in "KQRV" for g in range(NG)]
        counts = (2, 1, 2, 2, 1, 1, 1, 1, 1)
    else:
        fill = [("M", head + 1, kind, g) for kind in "KQV" for g in range(NG)]
        counts = (1,) * 9
    steps = [("S", 0, 8), ("S", 0, 0), ("P", 0, 8)] if head == 0 else []
    rotated = []
    for k, count in enumerate(counts):
        tile = order[k][1]
        if k + 1 < len(order):
            steps.append(("P", *order[k + 1]))
        steps.append(("T", head, tile))
        if k == 0 and head:
            steps.append(("O", head - 1, 3))
        elif k == 1 or k and tile % 2 == 0:
            steps.append(("O", head, 4 if k == 1 else tile // 2 - 1))
        steps += [("D", *unit) for unit in rotated]
        rotated = []
        if k + 2 < len(order):
            steps.append(("S", *order[k + 2]))
        for _ in range(count):
            what, h, kind, g = fill.pop(0)
            steps.append(("F", what, h, kind, g))
            if kind == "R":
                rotated.append((h, g))
    return steps + ([("O", head, 3)] if head + 1 == MH else [])


RET_UNITS = [(kind, g) for kind in "QK" for g in range(NG)] + [("V", t) for t in range(9)]


def retention_steps(head):
    fill = [("R", head + 1, *unit) for unit in RET_UNITS] if head + 1 < RH else []
    steps = [("A", 0)]
    for c in range(9):
        if fill:
            steps.append(("F", *fill.pop(0)))
        steps.append(("B", c))
        if c < 8:
            steps.append(("A", c + 1))
        steps.append(("N", c))
        if fill:
            steps.append(("F", *fill.pop(0)))
        if c:
            steps.append(("Z", c - 1))
    steps.append(("Z", 8))
    return steps + [("F", *unit) for unit in fill]


def keys_of(tile):
    return (0, (tile + 1) * P, P) if tile < 8 else (SEQ, DEC + PAST, DEC)


def build(nc, a, o):
    with ExitStack() as ctx:
        base = (nc.sbuf_base + 63) // 64 * 64

        def at(name, offset, shape, dt=F32):
            return nc.alloc_sbuf_tensor_at(name, [P, *shape], dt, offset=base + offset)

        def sem(name):
            return ctx.enter_context(nc.semaphore(name))

        stage = [at(f"w_stage{s}", 4096 * s, [8, P]) for s in range(2)]
        w_hi = at("w_hi", 8192, [2, 8, P], F32R)
        w_lo = at("w_lo", 16384, [2, 8, P], F32R)
        w_full = at("w_full", 8192, [2, 8, P])
        TMP = 24576
        tmp = [at(f"tmp{k}", TMP + WIDE * 4 * k, [WIDE]) for k in range(6)]
        CON = TMP + 6 * WIDE * 4
        eye = at("eye", CON, [P])
        ones = at("ones", CON + 512, [P])
        eps = at("eps", CON + 1216, [1])
        gains = at("gains", CON + 1024, [38])
        negmax = at("negmax", CON + 1280, [2, 2])
        rowsum = at("rowsum", CON + 1344, [2, 2])
        bnst = at("bnst", CON + 1408, [2, 6])
        mv = at("mv", CON + 1472, [2, 2])
        rstd = at("rstd", CON + 1536, [2, 1])
        half = at("half", CON + 1600, [1])
        veps = at("veps", CON + 1632, [2, 1])
        dmask = at("dmask", CON + 1664, [RH, P])
        dcol = at("dcol", CON + 3712, [RH, 3])
        G_MIX, G_Q, G_KV, G_GN, G_F, G_FIN = 0, 8, 12, 14, 22, 30
        M = CON + 4096

        def region(name, units, shape, dt=F32, extra=0):
            return at(name, M + int(units * U) // 64 * 64 + extra, shape, dt)

        xn_hi = region("xn_hi", 0, [KT, TOK], F32R)
        xn_lo = region("xn_lo", 8, [KT, TOK], F32R)
        xt = region("xt", 0, [KT, TOK])
        xa_hi = region("xa_hi", 16, [KT, TOK], F32R)
        xa_lo = region("xa_lo", 24, [KT, TOK], F32R)
        sumsq = region("sumsq", 10.75, [TOK])
        inv = region("inv", 11.75, [TOK])
        square = region("square", 12.75, [2, TOK])
        cq_raw = region("cq_raw", 32, [4, TOK])
        ckv_raw = region("ckv_raw", 36, [2, TOK])
        kpe_out = region("kpe_out", 15, [TOK])
        kp_hi = region("kp_hi", 25.6, [KEYS], F32R)
        kp_lo = region("kp_lo", 25.6, [KEYS], F32R, extra=KEYS * 4)
        cos64 = region("cos64", 38, [TOK])
        sin64 = region("sin64", 39, [TOK])
        cqn_hi = region("cqn_hi", 0, [4, TOK], F32R)
        cqn_lo = region("cqn_lo", 4, [4, TOK], F32R)
        ckn = region("ckn", 8, [2, KEYS])
        cpe_in = region("cpe_in", 10.5, [PAST])
        K_B, V_B = KEYS * 4, 11 * VD * 4
        k_hi = [region(f"k_hi{b}", (12.5, 16)[b], [KEYS], F32R) for b in range(2)]
        k_lo = [region(f"k_lo{b}", (12.5, 16)[b], [KEYS], F32R, extra=K_B) for b in range(2)]
        v_hi = [region(f"v_hi{b}", (18.5, 21.1)[b], [11, VD], F32R) for b in range(2)]
        v_lo = [region(f"v_lo{b}", (18.5, 21.1)[b], [11, VD], F32R, extra=V_B) for b in range(2)]
        p_exp = [region(f"p_exp{b}", 23.7, [SEQ], extra=4096 * b) for b in range(2)]
        q_hi = [region(f"q_hi{b}", 28.1 + 2 * b, [TOK], F32R) for b in range(2)]
        q_lo = [region(f"q_lo{b}", 29.1 + 2 * b, [TOK], F32R) for b in range(2)]
        qr = [[region(f"qr{p}{b}", (32.1, 10.48)[p] + b, [TOK], F32R) for b in range(2)] for p in range(2)]
        pt_hi = region("pt_hi", 34.15, [8, 2 * P], F32R)
        pt_lo = region("pt_lo", 34.15, [8, 2 * P], F32R, extra=8192)
        out_hl = [at(f"out_hl{b}", TMP + 5120 + 2048 * b, [2, 2 * P], F32R) for b in range(2)]
        rq = [region(f"rq{b}", 28.1 + 2 * b, [TOK]) for b in range(2)]
        rk = [region(f"rk{b}", 29.1 + 2 * b, [TOK]) for b in range(2)]
        rv = [region(f"rv{b}", (18.5, 21.1)[b], [9, DV]) for b in range(2)]
        cos128 = region("cos128", 38, [TOK])
        sin128 = region("sin128", 39, [TOK])
        R0 = int(34.15 * U) // 64 * 64

        def scratch(name, offset, shape):
            return region(name, 0, shape, extra=R0 + offset)

        st_f = [scratch(f"st_f{b}", 512 * b, [P]) for b in range(2)]
        kd_f = [scratch(f"kd_f{b}", 1024 + 512 * b, [P]) for b in range(2)]
        s_prompt = [scratch(f"s_prompt{b}", 2048 + 1024 * b, [DV]) for b in range(2)]
        s_sample = [scratch(f"s_sample{b}", 4096 + 1024 * b, [DV]) for b in range(2)]
        zs = [scratch(f"zs{b}", 6144 + 1024 * b, [DV]) for b in range(2)]
        zn = [scratch(f"zn{b}", 8192 + 1024 * b, [DV]) for b in range(2)]
        zt = [scratch(f"zt{b}", 10240 + 1024 * b, [2, P]) for b in range(2)]
        y_hi = region("y_hi", 16, [8, TOK], F32R)
        y_lo = region("y_lo", 24, [8, TOK], F32R)
        res = region("res", 32, [8, TOK])
        res_sq = region("res_sq", 22, [TOK])
        res_inv = region("res_inv", 23, [TOK])
        norm_f = [region(f"norm_f{b}", 18 + b, [TOK]) for b in range(2)]

        ps = ctx.enter_context(nc.psum_tensor("ps", [P, 8, 512], F32))

        xn_spill = nc.dram_tensor("xn_spill", (P, 2, KT, TOK), F32, kind="Internal").ap()
        ym_spill = nc.dram_tensor("ym_spill", (MH, P, 2, TOK), F32, kind="Internal").ap()
        yr_spill = nc.dram_tensor("yr_spill", (8, P, TOK), F32, kind="Internal").ap()

        stage_in = [sem("stage_in0"), sem("stage_in1")]
        w_high = sem("w_high")
        w_low = sem("w_low")
        consts_in = sem("consts_in")
        x_in = [sem(f"x_in{t}") for t in range(KT)]
        tables_in = sem("tables_in")
        cache_landed = sem("cache_landed")
        cache_ckv_in = sem("cache_ckv_in")
        cache_high = sem("cache_high")
        cache_low = sem("cache_low")
        kv_out = sem("kv_out")
        set_up = sem("set_up")
        squared = sem("squared")
        summed = sem("summed")
        stat_done = sem("stat_done")
        root_done = sem("root_done")
        inv_done = sem("inv_done")
        scaled = sem("scaled")
        norm_high = sem("norm_high")
        norm_low = [sem("norm_low_even"), sem("norm_low_odd")]
        g_done = sem("g_done")
        g_act = sem("g_act")
        g_free = sem("g_free")
        g_high = sem("g_high")
        g_low = sem("g_low")
        p_done = sem("p_done")
        p_high = sem("p_high")
        p_free = sem("p_free")
        rot_sum = sem("rot_sum")
        rot_high = sem("rot_high")
        rot_low = sem("rot_low")
        v_chain = sem("v_chain")
        pool_chain = sem("pool_chain")
        s_done = sem("s_done")
        max_done = sem("max_done")
        exp_done = sem("exp_done")
        prob_done = sem("prob_done")
        t_done = sem("t_done")
        t_high = sem("t_high")
        t_low = sem("t_low")
        o_out = [sem("o_out0"), sem("o_out1")]
        pt_zero = sem("pt_zero")
        kd_done = sem("kd_done")
        kd_copy = sem("kd_copy")
        sc_done = sem("sc_done")
        sc_mid = sem("sc_mid")
        z_done = sem("z_done")
        z_copy = sem("z_copy")
        z_stat = sem("z_stat")
        z_rstd = sem("z_rstd")
        z_norm = sem("z_norm")
        zt_done = sem("zt_done")
        zt_copy = sem("zt_copy")
        zt_out = [sem("zt_out0"), sem("zt_out1")]
        u_done = sem("u_done")
        state_zero = sem("state_zero")
        state_f = sem("state_f")
        state_in = [sem("state_in0"), sem("state_in1")]
        state_out = [sem("state_out0"), sem("state_out1")]
        spill_out = sem("spill_out")
        xn_in = [sem(f"xn_in{t}") for t in range(KT)]
        yr_in = [sem("yr_in0"), sem("yr_in1")]
        ym_in = [sem(f"ym_in{t}") for t in range(KT)]
        m_add = sem("m_add")
        split_hi = sem("split_hi")
        split_lo = sem("split_lo")
        xres_in = [sem("xres_in0"), sem("xres_in1")]
        out_done = sem("out_done")

        W = a["weights"]
        def s_index(h, tile):
            return 9 * h + (0 if tile == 8 else tile + 1)

        T_UNITS = [1] + [t // 4 + 1 for t in range(8)]
        T_HEAD = sum(T_UNITS)

        def t_index(h, tile):
            pos = 0 if tile == 8 else tile + 1
            return T_HEAD * h + sum(T_UNITS[:pos])

        def t_blocks(tile):
            n = tile + 1 if tile < 8 else 3
            return [(k, min(4, n - k)) for k in range(0, n, 4)]

        def o_index(h, pair):
            return 5 * h + (0 if pair == 4 else pair + 1)

        p_order = {}
        for g in range(NG * 4):
            p_order["M", 0, "KQRV"[g // NG], g % NG] = len(p_order)
        for h in range(MH):
            for s in attention_steps(h):
                if s[0] == "F":
                    p_order[s[1:]] = len(p_order)
                if s[0] == "O":
                    p_order["M", s[1], "O", s[2]] = len(p_order)
        for h in range(RH):
            for s in retention_steps(h):
                if s[0] == "F":
                    p_order[s[1:]] = len(p_order)
        ATT_END = p_order["M", MH - 1, "O", 3] + 1
        rotated = [k for k in p_order if (k[0] == "M" and k[2] == "R") or (k[0] == "R" and k[2] in "QK")]
        rot_index = {k: i + NG for i, k in enumerate(rotated)}
        ROT_MLA = NG + NG * MH // 2
        high_index = {k: i for i, k in enumerate(
            [k for k in p_order if k[0] == "M" and k[2] != "R"])}

        def t_end(n):
            return T_HEAD * (n // 9) + sum(T_UNITS[:n % 9 + 1])

        F_A, F_GATE = 0, 3 * N_A
        F_M1, A_M1 = F_GATE + 24, 24
        F_M2, A_M2 = F_M1 + 24, A_M1 + 24
        F_OUT, F_FFN, A_FFN = F_M2 + 24, F_M2 + 48, A_M2 + 24
        SUM_OUT, SUM_FIN = KT + 6, KT + 6 + 24

        def mla_item(h, kind):
            pair = I_MLA + 3 * (h // 2)
            if kind == "R":
                return pair + 1
            return pair + (2 if h % 2 else 0)

        def ret_item(h, kind):
            return I_RET + 4 * h + {"Q": 0, "K": 1, "V": 2}[kind]

        def full_blocks(n):
            return 4 if n is not None and I_MLA <= n < I_RET and (n - I_MLA) % 3 != 1 else 0

        rot_cos, rot_sin, rot_total = tmp[0], tmp[1], tmp[2]
        root = (tmp[2], tmp[3])

        def wait_low(engine, k):
            engine.wait_ge(norm_low[k % 2], k // 2 + 1)

        block = ctx.enter_context(nc.Block())

        @block.sync
        def _(sp):
            def load_item(n):
                sp.dma_start(stage[n % 2][:, :, :], W[n]).then_inc(stage_in[n % 2], 16)

            def items(first, last):
                for n in range(first, last):
                    sp.wait_ge(w_low, n - 1)
                    load_item(n)

            def item_in_loop(i, n):
                sp.wait_ge(w_low, 2 * i + (n - 1))
                sp.dma_start(stage[n % 2][:, :, :], W[2 * i + n]).then_inc(stage_in[n % 2], 16)

            for t in range(KT):
                sp.dma_start(xt[:, t, :], a["x"][:, t, :]).then_inc(x_in[t], 16)
            for name, dst in (("eye", eye[:, :]), ("gains", gains[:, :]), ("dmask", dmask[:, :, :]),
                              ("dcol", dcol[:, :, :])):
                sp.dma_start(dst, a[name]).then_inc(consts_in, 16)
            load_item(0)
            load_item(1)
            sp.dma_start(cos64[:, :], a["cos64"]).then_inc(tables_in, 16)
            sp.dma_start(sin64[:, :], a["sin64"]).then_inc(tables_in, 16)
            for t in range(KT):
                wait_low(sp, t)
                sp.dma_start(xn_spill[:, 0, t, :], xa_hi[:, t, :].bitcast(F32)).then_inc(spill_out, 16)
                sp.dma_start(xn_spill[:, 1, t, :], xa_lo[:, t, :].bitcast(F32)).then_inc(spill_out, 16)
            sp.dma_start(cpe_in[0:ROPE, :], a["cache_kpe"]).then_inc(cache_landed, 16)
            sp.dma_start(ckn[:, :, TOK:KEYS], a["cache_ckv"]).then_inc(cache_ckv_in, 16)
            items(2, I_MLA + 2)
            sp.wait_ge(rot_sum, NG)
            sp.dma_start(o["kpe"], kpe_out[0:ROPE, 0:TOK]).then_inc(kv_out, 16)
            sp.wait_ge(scaled, KT + 6)
            sp.dma_start(o["ckv"], ckn[:, :, 0:TOK]).then_inc(kv_out, 16)
            items(I_MLA + 2, I_MLA + 4)

            def items_ahead(what, h, kind, g):
                if g == 0 and what == "M" and kind in "KR":
                    items(mla_item(h, kind) + 2, mla_item(h, kind) + 3)
                if g == 0 and what == "R":
                    n = ret_item(h, kind) + 2
                    items(n, n + (2 if kind == "V" else 1))

            for h in range(MH):
                for k, s in enumerate(attention_steps(h)):
                    if h == MH - 1 and k == 0:
                        sp.wait_ge(p_free, p_order["M", MH - 2, "O", 3] + 1)
                        sp.wait_ge(kv_out, 32)
                        for t in range(KT):
                            sp.dma_start(xn_hi[:, t, :].bitcast(F32), xn_spill[:, 0, t, :]).then_inc(xn_in[t], 16)
                            sp.dma_start(xn_lo[:, t, :].bitcast(F32), xn_spill[:, 1, t, :]).then_inc(xn_in[t], 16)
                            if t == 0:
                                sp.dma_start(cos128[:, :], a["cos128"]).then_inc(tables_in, 16)
                                sp.dma_start(sin128[:, :], a["sin128"]).then_inc(tables_in, 16)
                    if s[0] == "F":
                        items_ahead(*s[1:])
                    if s[0] == "O":
                        of_head, pair = s[1:]
                        n = o_index(of_head, pair)
                        c0, c1 = (SEQ, TOK) if pair == 4 else (pair * 2 * P, (pair + 1) * 2 * P)
                        sp.wait_ge(p_free, p_order["M", of_head, "O", pair] + 1)
                        sp.dma_start(ym_spill[of_head, :, :, c0:c1],
                                     out_hl[n % 2][:, :, 0:c1 - c0].bitcast(F32)).then_inc(o_out[n % 2], 16)
            def state_load(h):
                sp.dma_start(s_sample[h % 2][:, :], a["state"][:, h, :]).then_inc(state_in[h % 2], 16)

            state_load(0)
            state_load(1)
            for h in range(RH):
                for s in retention_steps(h):
                    if s[0] == "F":
                        items_ahead(*s[1:])
                    if s == ("A", 8):
                        sp.wait_ge(state_f, 9 * h + 8)
                        sp.dma_start(o["state_p"][:, h, :], s_prompt[h % 2][:, :]).then_inc(state_out[h % 2], 16)
                    if s[0] == "Z":
                        n = 9 * h + s[1]
                        c0, c1 = s[1] * P, min(TOK, (s[1] + 1) * P)
                        sp.wait_ge(zt_copy, n + 1)
                        for j in range(2):
                            sp.dma_start(yr_spill[2 * h + j, :, c0:c1],
                                         zt[n % 2][:, j, 0:c1 - c0]).then_inc(zt_out[n % 2], 16)
                sp.wait_ge(state_f, 9 * h + 9)
                sp.dma_start(o["state_s"][:, h, :], s_sample[h % 2][:, :]).then_inc(state_out[h % 2], 16)
                if h + 2 < RH:
                    sp.wait_ge(state_out[h % 2], 32 * (h // 2 + 1))
                    state_load(h + 2)
            for b in range(2):
                sp.wait_ge(zt_out[b], 32 * 18)
            sp.wait_ge(rot_sum, NG + len(rotated))
            with sp.Fori(0, 4) as i:
                for j in range(2):
                    for g, (c0, c1) in enumerate(GROUPS):
                        k = 3 * j + g
                        sp.wait_ge(g_free, 6 * i + (F_GATE + k - 1))
                        sp.dma_start(tmp[k % 2][:, 0:c1 - c0], yr_spill[2 * i + j, :, c0:c1])\
                          .then_inc(yr_in[k % 2], 16)
                    item_in_loop(i, I_GATE + 2 + j)
            with sp.Fori(0, 8) as i:
                for j in range(2):
                    item_in_loop(i, I_M1 + 2 + j)
            for b in range(2):
                sp.wait_ge(o_out[b], 16 * 20)
            sp.wait_ge(g_done, G_M2)
            for t in range(KT):
                sp.dma_start(y_hi[:, t, :].bitcast(F32), ym_spill[t, :, 0, :]).then_inc(ym_in[t], 16)
                sp.dma_start(y_lo[:, t, :].bitcast(F32), ym_spill[t, :, 1, :]).then_inc(ym_in[t], 16)
            with sp.Fori(0, 8) as i:
                for j in range(2):
                    item_in_loop(i, I_M2 + 2 + j)
            with sp.Fori(0, 4) as i:
                for j in range(2):
                    for g, (c0, c1) in enumerate(GROUPS):
                        k = 3 * j + g
                        sp.wait_ge(g_free, 6 * i + (F_OUT + k - 1))
                        sp.dma_start(tmp[k % 2][:, 0:c1 - c0], a["x"][:, 2 * i + j, c0:c1])\
                          .then_inc(xres_in[k % 2], 16)
                    item_in_loop(i, I_OUT + 2 + j)
            with sp.Fori(0, (N_ITEMS - I_FFN) // 2 - 1) as i:
                for j in range(2):
                    item_in_loop(i, I_FFN + 2 + j)
            for t in range(KT):
                sp.wait_ge(scaled, 2 * KT + 6 + t + 1)
                sp.dma_start(o["y"][:, t, :], res[:, t, :]).then_inc(out_done, 16)
            for b in range(2):
                sp.wait_ge(state_out[b], 16 * RH)
            sp.wait_ge(kv_out, 32)
            sp.wait_ge(out_done, 16 * KT)

        @block.tensor
        def _(pe):
            def product(out, wh, wl, xh, xl, start=True, stop=True):
                nc.tensor.matmul(out, wh, xh, start=start, stop=False)
                nc.tensor.matmul(out, wl, xh, start=False, stop=False)
                return nc.tensor.matmul(out, wh, xl, start=False, stop=stop)

            def block_product(slot, k, g, bank, hi, lo, blocks, rows):
                c0, c1 = GROUPS[g]
                return product(ps[0:rows, bank + g, 0:c1 - c0], w_hi[:, slot, k, 0:rows], w_lo[:, slot, k, 0:rows],
                               hi[:, k, c0:c1], lo[:, k, c0:c1], k == 0, k == blocks - 1)

            def item_units(slot, n, bank, free, hi, lo, blocks=8, rows=P, between=None):
                pe.wait_ge(w_low, n + 1)
                for g in range(NG):
                    if free is not None:
                        pe.wait_ge(free[0], free[1] + g)
                    for k in range(blocks):
                        last = block_product(slot, k, g, bank, hi, lo, blocks, rows)
                    last.then_inc(g_done, 1)
                    if between is not None and g == 0:
                        between()

            def streamed_item(slot, n, bank, free, hi, lo, ready):
                pe.wait_ge(w_low, n + 1)
                if free is not None:
                    pe.wait_ge(free[0], free[1] + NG - 1)
                for k in range(KT - 2):
                    ready(k)
                    for g in range(NG):
                        block_product(slot, k, g, bank, hi, lo, KT, P)
                for g in range(NG):
                    for k in (KT - 2, KT - 1):
                        if g == 0:
                            ready(k)
                        last = block_product(slot, k, g, bank, hi, lo, KT, P)
                    last.then_inc(g_done, 1)

            def feature_sums(k, src):
                for g, (c0, c1) in enumerate(GROUPS):
                    m = 3 * k + g
                    if m >= 2:
                        pe.wait_ge(root_done, m - 1)
                    nc.tensor.matmul(ps[:, 6 + m % 2, 0:c1 - c0], ones[:, :], src[:, c0:c1],
                                     start=True, stop=True).then_inc(stat_done, 1)

            pe.wait_ge(summed, KT)
            feature_sums(0, sumsq)
            streamed_item(I_A % 2, I_A, 0, None, xa_hi, xa_lo, lambda k: wait_low(pe, k))

            def kv_sums():
                pe.wait_ge(summed, KT + 6)
                feature_sums(2, sumsq)

            for j in range(1, N_A):
                n = I_A + j
                last_item = j == N_A - 1
                item_units(n % 2, n, 3 * (j % 2), None if j < 2 else (g_free, 3 * j - 5), xa_hi, xa_lo,
                           rows=ROPE if last_item else P, between=kv_sums if last_item else None)
                if j == 4:
                    pe.wait_ge(summed, KT + 4)
                    feature_sums(1, sumsq)

            def projection(h, kind, g):
                b, key = h % 2, ("M", h, kind, g)
                u = p_order[key]
                bank = 6 + u % 2
                n = mla_item(h, kind)
                slot = n % 2
                pe.wait_ge(w_low, n + 1)
                if u >= 2:
                    pe.wait_ge(p_free, u - 1)
                if kind == "K":
                    c0, c1 = KEY_GROUPS[g]
                    for k in range(2):
                        last = nc.tensor.matmul(ps[:, bank, 0:c1 - c0], w_full[:, slot, k, :],
                                                ckn[:, k, c0:c1], start=k == 0, stop=k == 1)
                elif kind == "V":
                    for t in range(4 * g, min(11, 4 * g + 4)):
                        c0, c1 = t * P, min(KEYS, (t + 1) * P)
                        for k in range(2):
                            last = nc.tensor.matmul(ps[0:c1 - c0, bank, (t % 4) * P:(t % 4 + 1) * P],
                                                    ckn[:, k, c0:c1], w_full[:, slot, 2 + k, :],
                                                    start=k == 0, stop=k == 1)
                else:
                    c0, c1 = GROUPS[g]
                    first = 4 if kind == "Q" else 0
                    for k in range(4):
                        last = product(ps[:, bank, 0:c1 - c0], w_hi[:, slot, first + k, :],
                                       w_lo[:, slot, first + k, :],
                                       cqn_hi[:, k, c0:c1], cqn_lo[:, k, c0:c1], k == 0, k == 3)
                last.then_inc(p_done, 1)

            wait_low(pe, KT + 2)
            wait_low(pe, KT + 3)
            pe.wait_ge(scaled, KT + 6)
            pe.wait_ge(cache_ckv_in, 16)
            pe.wait_ge(root_done, 9)
            def ret_projection(h, kind, g):
                b = h % 2
                u = p_order["R", h, kind, g]
                bank = 6 + u % 2
                pe.wait_ge(p_free, u - 1)
                n = ret_item(h, kind)
                pe.wait_ge(w_low, n + (2 if kind == "V" else 1))
                if kind in "QK":
                    c0, c1 = GROUPS[g]
                    for k in range(KT):
                        if h == 0 and kind == "Q" and g == 0:
                            pe.wait_ge(xn_in[k], 32)
                        last = product(ps[:, bank, 0:c1 - c0], w_hi[:, n % 2, k, :], w_lo[:, n % 2, k, :],
                                       xn_hi[:, k, c0:c1], xn_lo[:, k, c0:c1], k == 0, k == KT - 1)
                else:
                    c0, c1 = g * P, min(TOK, (g + 1) * P)
                    out = ps[0:c1 - c0, bank, 0:DV].rearrange("p (s n) -> p s n", s=2)
                    for k in range(KT):
                        last = product(out, xn_hi[:, k, c0:c1], xn_lo[:, k, c0:c1],
                                       w_hi[:, :, k, :], w_lo[:, :, k, :], k == 0, k == KT - 1)
                last.then_inc(p_done, 1)

            def fill(what, h, kind, g):
                (projection if what == "M" else ret_projection)(h, kind, g)

            for kind in "KQRV":
                for g in range(NG):
                    projection(0, kind, g)
            pe.wait_ge(cache_low, 1)
            pe.wait_ge(rot_low, NG)
            pe.wait_ge(g_free, F_GATE)
            for head in range(MH):
                for s in attention_steps(head):
                    if s[0] == "F":
                        fill(*s[1:])
                        continue
                    h, tile = s[1:]
                    b = h % 2
                    if s[0] == "S":
                        rotary = qr[(h // 2 + 1) % 2][b]
                        n = s_index(h, tile)
                        key0, nk, nq = keys_of(tile)
                        if tile == 8:
                            if h % 2 == 0:
                                pe.wait_ge(rot_low, 1 + rot_index["M", h, "R", NG - 1])
                            pe.wait_ge(p_free, 1 + p_order["M", h, "Q", NG - 1])
                        if n >= 2:
                            pe.wait_ge(exp_done, n - 1)
                        q0 = tile * P
                        for c in range(0, nk, 512):
                            w = max(2 * P, min(512, nk - c))
                            out = ps[0:nq, 2 * (n % 2) + c // 512, 0:w]
                            keys = slice(key0 + c, key0 + c + w)
                            product(out, q_hi[b][:, q0:q0 + nq], q_lo[b][:, q0:q0 + nq],
                                    k_hi[b][:, keys], k_lo[b][:, keys], True, False)
                            nc.tensor.matmul(out, rotary[:, q0:q0 + nq], kp_hi[:, keys], start=False, stop=False)
                            last = nc.tensor.matmul(out, rotary[:, q0:q0 + nq], kp_lo[:, keys],
                                                    start=False, stop=True)
                        last.then_inc(s_done, 1)
                    elif s[0] == "T":
                        n = s_index(h, tile)
                        _, nk, nq = keys_of(tile)
                        pe.wait_ge(prob_done, n + 1)
                        for i, (k0, nb) in enumerate(t_blocks(tile)):
                            t = t_index(h, tile) + i
                            if t >= 2:
                                pe.wait_ge(t_low, t - 1)
                            for k in range(nb):
                                w = min(P, nk - (k0 + k) * P)
                                last = nc.tensor.transpose(
                                    ps[0:w, 4 + t % 2, k * P:k * P + nq],
                                    p_exp[n % 2][0:nq, (k0 + k) * P:(k0 + k) * P + w], eye[0:nq, 0:nq])
                            last.then_inc(t_done, 1)
                    elif s[0] == "O":
                        pair = s[2]
                        u = p_order["M", h, "O", pair]
                        if pair == 4:
                            pe.wait_ge(p_free, p_order["M", h, "V", NG - 1] + 1)
                        pe.wait_ge(t_low, t_index(h, 8 if pair == 4 else 2 * pair + 1)
                                   + len(t_blocks(8 if pair == 4 else 2 * pair + 1)))
                        pe.wait_ge(p_free, u - 1)
                        if pair == 0:
                            pe.wait_ge(pt_zero, h + 1)
                        nkt = 3 if pair == 4 else 2 * pair + 2
                        lo, hi = (P, P + DEC) if pair == 4 else (0, 2 * P)
                        for kt in range(nkt):
                            vt = 8 + kt if pair == 4 else kt
                            rows = DEC if vt == 10 else P
                            last = product(ps[:, 6 + u % 2, 0:hi - lo], v_hi[b][0:rows, vt, :], v_lo[b][0:rows, vt, :],
                                           pt_hi[0:rows, kt, lo:hi], pt_lo[0:rows, kt, lo:hi],
                                           kt == 0, kt == nkt - 1)
                        last.then_inc(p_done, 1)

            for h in range(RH):
                b = h % 2
                for s in retention_steps(h):
                    if s[0] == "F":
                        fill(*s[1:])
                        continue
                    c = s[1]
                    n = 9 * h + c
                    c0, c1 = c * P, min(TOK, (c + 1) * P)
                    L = c1 - c0
                    if s[0] == "A":
                        if c == 0:
                            pe.wait_ge(rot_sum, 1 + rot_index["R", h, "K", NG - 1])
                            pe.wait_ge(p_free, 1 + p_order["R", h, "V", 8])
                        if n:
                            pe.wait_ge(kd_copy, n)
                        nc.tensor.transpose(ps[0:L, 3, 0:DK], rk[b][:, c0:c1], eye[:, :]).then_inc(kd_done, 1)
                        if n:
                            pe.wait_ge(sc_mid, n)
                        nc.tensor.matmul(ps[0:L, 0, 0:L], rk[b][:, c0:c1], rq[b][:, c0:c1],
                                         start=True, stop=True).then_inc(sc_done, 1)
                    elif s[0] == "B":
                        state = s_prompt[b] if c < 8 else s_sample[b]
                        if c == 0:
                            pe.wait_ge(state_zero, h + 1)
                        elif c == 8:
                            pe.wait_ge(state_in[b], 16 * (h // 2 + 1))
                        if n:
                            pe.wait_ge(state_f, n)
                            pe.wait_ge(z_copy, n)
                        pe.wait_ge(sc_mid, n + 1)
                        out = ps[0:L, 1, 0:DV]
                        nc.tensor.matmul(out, rq[b][:, c0:c1], state[:, :], start=True, stop=False)
                        nc.tensor.matmul(out, st_f[n % 2][0:L, 0:L], rv[b][0:L, c, :],
                                         start=False, stop=True).then_inc(z_done, 1)
                        pe.wait_ge(kd_copy, n + 1)
                        nc.tensor.matmul(ps[:, 4, 0:DV], kd_f[n % 2][0:L, :], rv[b][0:L, c, :],
                                         start=True, stop=True).then_inc(u_done, 1)
                    elif s[0] == "Z":
                        pe.wait_ge(z_norm, n + 1)
                        if n:
                            pe.wait_ge(zt_copy, n)
                        for j in range(2):
                            last = nc.tensor.transpose(ps[:, 2, j * P:j * P + L],
                                                       zn[n % 2][0:L, j * P:(j + 1) * P], eye[0:L, 0:L])
                        last.then_inc(zt_done, 1)

            pe.wait_ge(zt_copy, 9 * RH)
            pe.wait_ge(state_f, 9 * RH)
            with pe.Fori(0, 4) as i:
                for j in range(2):
                    item_units((I_GATE + j) % 2, 2 * i + (I_GATE + j), 3 * j,
                               (g_free, 6 * i + (F_GATE + 3 * j - 5)), xn_hi, xn_lo)
            pe.wait_ge(g_low, 24)
            for n0, free0, act0, branch in ((I_M1, F_M1, A_M1, 0), (I_M2, F_M2, A_M2, 1)):
                if branch:
                    item_units(n0 % 2, n0, 0, (g_act, act0 - 2), xn_hi, xn_lo)
                    streamed_item((n0 + 1) % 2, n0 + 1, 3, (g_free, free0 - 2), y_hi, y_lo,
                                  lambda k: pe.wait_ge(ym_in[k], 32))
                with pe.Fori(branch, 8) as i:
                    item_units(n0 % 2, 2 * i + n0, 0, (g_act, 3 * i + (act0 - 2)), xn_hi, xn_lo)
                    item_units((n0 + 1) % 2, 2 * i + (n0 + 1), 3, (g_free, 3 * i + (free0 - 2)), y_hi, y_lo)
            streamed_item(I_OUT % 2, I_OUT, 0, (g_free, F_OUT - 5), xn_hi, xn_lo,
                          lambda k: pe.wait_ge(split_lo, k + 1))
            item_units((I_OUT + 1) % 2, I_OUT + 1, 3, (g_free, F_OUT - 2), xn_hi, xn_lo)
            with pe.Fori(1, 4) as i:
                for j in range(2):
                    item_units((I_OUT + j) % 2, 2 * i + (I_OUT + j), 3 * j,
                               (g_free, 6 * i + (F_OUT + 3 * j - 5)), xn_hi, xn_lo)

            pe.wait_ge(summed, SUM_OUT + 24)
            feature_sums(3, res_sq)
            n0, free0, act0, low0 = I_FFN, F_FFN, A_FFN, 24
            for f, (_, tiles) in enumerate(FFN_GROUPS):
                pe.wait_ge(g_free, free0 - 3)
                if f == 0:
                    streamed_item(n0 % 2, n0, 0, (g_act, act0 - 2), xn_hi, xn_lo,
                                  lambda k: wait_low(pe, KT + 4 + k))
                    item_units((n0 + 1) % 2, n0 + 1, 3, (g_free, free0 - 2), xn_hi, xn_lo)
                with pe.Fori(1 if f == 0 else 0, tiles) as i:
                    item_units(n0 % 2, 2 * i + n0, 0, (g_act, 3 * i + (act0 - 2)), xn_hi, xn_lo)
                    item_units((n0 + 1) % 2, 2 * i + (n0 + 1), 3, (g_free, 3 * i + (free0 - 2)), xn_hi, xn_lo)
                n0, free0, act0, low0 = n0 + 2 * tiles, free0 + 3 * tiles, act0 + 3 * tiles, low0 + 3 * tiles
                pe.wait_ge(g_low, low0)
                with pe.Fori(0, 4) as i:
                    for j in range(2):
                        item_units((n0 + j) % 2, 2 * i + (n0 + j), 3 * j,
                                   (g_free, 6 * i + (free0 + 3 * j - 5)), y_hi, y_lo, blocks=tiles)
                n0, free0 = n0 + 8, free0 + 24
            pe.wait_ge(summed, SUM_FIN + 24)
            feature_sums(4, res_sq)

        @block.scalar
        def _(act):
            def split_high(slot, n, turn):
                act.wait_ge(stage_in[slot], 16 * turn + 16)
                first = full_blocks(n)
                if first:
                    nc.scalar.activation(w_full[:, slot, 0:first, :], stage[slot][:, 0:first, :], ACT.Copy)
                nc.scalar.activation(w_hi[:, slot, first:8, :], stage[slot][:, first:8, :],
                                     ACT.Copy).then_inc(w_high, 1)

            def item(n):
                split_high(n % 2, n, n // 2)

            def in_loop(i, n1):
                split_high(n1 % 2, None, i + n1 // 2)

            def squares(first, src, tiles):
                for t in tiles:
                    k = first + t
                    if first == 0:
                        act.wait_ge(x_in[t], 16)
                    if k >= 2:
                        act.wait_ge(summed, k - 1)
                    nc.scalar.activation(square[:, k % 2, :], src[:, t, :], ACT.Square).then_inc(squared, 1)

            def roots(k, width):
                for g, (c0, c1) in enumerate(GROUPS):
                    m = 3 * k + g
                    act.wait_ge(stat_done, m + 1)
                    if m >= 2:
                        act.wait_ge(inv_done, m - 1)
                    nc.scalar.activation(root[m % 2][:, 0:c1 - c0], ps[:, 6 + m % 2, 0:c1 - c0], ACT.Sqrt,
                                         bias=eps[:, :], scale=1.0 / width).then_inc(root_done, 1)

            def highs(first, dst, src, tiles):
                for t in tiles:
                    act.wait_ge(scaled, first + t + 1)
                    nc.scalar.activation(dst[:, t, 0:TOK], src[:, t, :], ACT.Copy).then_inc(norm_high, 1)

            squares(0, xt, range(KT))
            act.wait_ge(set_up, 1)
            roots(0, D_MODEL)
            item(0)
            highs(0, xa_hi, xt, range(KT))
            for j in range(N_A):
                if j == 4:
                    act.wait_ge(g_free, 12)
                    squares(KT, cq_raw, range(4))
                if j == 5:
                    roots(1, Q_LORA)
                    for t in range(KT):
                        wait_low(act, t)
                    highs(KT, cqn_hi, cq_raw, range(2))
                if j == 6:
                    act.wait_ge(g_free, 18)
                    squares(KT + 4, ckv_raw, range(2))
                act.wait_ge(g_done, G_A + 3 * j + 1)
                item(I_A + j + 1)
                if j == 5:
                    highs(KT, cqn_hi, cq_raw, range(2, 4))
            roots(2, KV_LORA)

            def shared_key():
                act.wait_ge(g_done, G_GATE)
                act.wait_ge(spill_out, 2 * KT * 16)
                for g, (c0, c1) in enumerate(GROUPS):
                    act.wait_ge(rot_sum, g + 1)
                    nc.scalar.activation(kp_hi[0:ROPE, c0:c1], kpe_out[0:ROPE, c0:c1], ACT.Copy)
                    nc.scalar.activation(kp_hi[ROPE:P, c0:c1], kpe_out[0:ROPE, c0:c1],
                                         ACT.Copy).then_inc(rot_high, 1)
                act.wait_ge(cache_landed, 16)
                nc.scalar.activation(kp_hi[0:ROPE, TOK:KEYS], cpe_in[0:ROPE, :], ACT.Copy)
                nc.scalar.activation(kp_hi[ROPE:P, TOK:KEYS], cpe_in[0:ROPE, :], ACT.Copy).then_inc(cache_high, 1)

            def projection(h, kind, g):
                b, key = h % 2, ("M", h, kind, g)
                u = p_order[key]
                if kind != "R":
                    act.wait_ge(p_done, u + 1)
                bank = 6 + u % 2
                if kind == "K":
                    c0, c1 = KEY_GROUPS[g]
                    nc.scalar.activation(k_hi[b][:, c0:c1], ps[:, bank, 0:c1 - c0], ACT.Copy).then_inc(p_high, 1)
                elif kind == "V":
                    full = 4 if g < 2 else 2
                    dst = v_hi[b][:, 4 * g:4 * g + full, :]
                    src = ps[:, bank, 0:full * P].rearrange("p (t e) -> p t e", t=full)
                    ins = nc.scalar.activation(dst, src, ACT.Copy)
                    if g == 2:
                        ins = nc.scalar.activation(v_hi[b][0:DEC, 10, :], ps[0:DEC, bank, 256:384], ACT.Copy)
                    ins.then_inc(p_high, 1)
                elif kind == "Q":
                    c0, c1 = GROUPS[g]
                    nc.scalar.activation(q_hi[b][:, c0:c1], ps[:, bank, 0:c1 - c0], ACT.Copy).then_inc(p_high, 1)
                n = mla_item(h, kind)
                if kind == "K" and g == 0:
                    item(n + 1)
                if kind == "V" and g == NG - 1 and h % 2 == 0:
                    item(n + 2)

            def rotary_parts(h, g):
                c0, c1 = GROUPS[g]
                rotary = qr[(h // 2 + 1) % 2]
                act.wait_ge(rot_sum, rot_index["M", h, "R", g] + 1)
                nc.scalar.activation(rotary[0][0:64, c0:c1], rot_total[0:64, 0:c1 - c0], ACT.Copy)
                nc.scalar.activation(rotary[1][64:128, c0:c1], rot_total[64:128, 0:c1 - c0],
                                     ACT.Copy).then_inc(rot_high, 1)

            def ret_projection(h, kind, g):
                u = p_order["R", h, kind, g]
                n = ret_item(h, kind)
                if kind in "QK" and g == 0:
                    act.wait_ge(p_done, u + 1)
                    item(n + 1)
                if kind == "K" and g == NG - 1:
                    act.wait_ge(p_done, u + 1)
                    item(n + 2)
                if kind == "V" and g == 8:
                    act.wait_ge(p_done, u + 1)
                    item(n + 2)

            def fill(what, h, kind, g):
                (projection if what == "M" else ret_projection)(h, kind, g)

            for kind in "KQRV":
                for g in range(NG):
                    projection(0, kind, g)
                    if kind == "R":
                        rotary_parts(0, g)
                if kind == "K":
                    shared_key()
            for head in range(MH):
                for s in attention_steps(head):
                    if s[0] == "F":
                        fill(*s[1:])
                        continue
                    h, tile = s[1:]
                    if s[0] == "D":
                        rotary_parts(*s[1:])
                    elif s[0] == "S":
                        n = s_index(h, tile)
                        _, nk, nq = keys_of(tile)
                        act.wait_ge(max_done, n + 1)
                        if n >= 2:
                            act.wait_ge(t_done, t_end(n - 2))
                        bank = 2 * (n % 2)
                        src = ps[0:nq, bank:bank + 2, :].rearrange("p b k -> p (b k)")[:, 0:nk]
                        nc.scalar.activation(p_exp[n % 2][0:nq, 0:nk], src, ACT.Exp,
                                             bias=negmax[0:nq, n % 2, 0:1], scale=SCALE,
                                             accum_out=rowsum[0:nq, n % 2, 0:1]).then_inc(exp_done, 1)
                    elif s[0] == "T":
                        _, nk, nq = keys_of(tile)
                        q0 = P * (tile % 2) if tile < 8 else P
                        for i, (k0, nb) in enumerate(t_blocks(tile)):
                            t = t_index(h, tile) + i
                            act.wait_ge(t_done, t + 1)
                            if i == 0 and (tile % 2 == 0) and (h or tile != 8):
                                act.wait_ge(p_done, 1 + (p_order["M", h - 1, "O", 3] if tile == 8 else
                                                     p_order["M", h, "O", tile // 2 - 1 if tile else 4]))
                            full = nb if tile < 8 else 2
                            src = ps[:, 4 + t % 2, 0:full * P].rearrange("p (k q) -> p k q", k=full)[:, :, 0:nq]
                            ins = nc.scalar.activation(pt_hi[:, k0:k0 + full, q0:q0 + nq], src, ACT.Copy)
                            if tile == 8:
                                ins = nc.scalar.activation(pt_hi[0:DEC, 2, q0:q0 + nq],
                                                           ps[0:DEC, 4 + t % 2, 2 * P:2 * P + nq], ACT.Copy)
                            ins.then_inc(t_high, 1)
                    elif s[0] == "O":
                        pair = s[2]
                        n = o_index(h, pair)
                        w = DEC if pair == 4 else 2 * P
                        u = p_order["M", h, "O", pair]
                        act.wait_ge(p_done, u + 1)
                        if n >= 2:
                            act.wait_ge(o_out[n % 2], 16 * (n // 2))
                        nc.scalar.activation(out_hl[n % 2][:, 0, 0:w], ps[:, 6 + u % 2, 0:w],
                                             ACT.Copy).then_inc(p_high, 1)

            for h in range(RH):
                for s in retention_steps(h):
                    if s[0] == "F":
                        fill(*s[1:])
                        continue
                    c = s[1]
                    n = 9 * h + c
                    L = P if c < 8 else DEC
                    if s[0] == "A":
                        col = 1 if c < 8 else 2
                        act.wait_ge(kd_done, n + 1)
                        if n >= 2:
                            act.wait_ge(u_done, n - 1)
                        nc.scalar.activation(kd_f[n % 2][0:L, :], ps[0:L, 3, 0:DK], ACT.Copy,
                                             scale=dcol[0:L, h, col:col + 1]).then_inc(kd_copy, 1)
                    elif s[0] == "B":
                        act.wait_ge(z_done, n + 1)
                        if n >= 2:
                            act.wait_ge(z_norm, n - 1)
                        nc.scalar.activation(zs[n % 2][0:L, :], ps[0:L, 1, 0:DV], ACT.Copy,
                                             scale=dcol[0:L, h, 0:1]).then_inc(z_copy, 1)
                    elif s[0] == "Z":
                        act.wait_ge(zt_done, n + 1)
                        if n >= 2:
                            act.wait_ge(zt_out[n % 2], 32 * (n // 2))
                        for j in range(2):
                            ins = nc.scalar.activation(zt[n % 2][:, j, 0:L], ps[:, 2, j * P:j * P + L], ACT.Copy,
                                                       scale=gains[:, G_GN + 2 * h + j:G_GN + 2 * h + j + 1])
                        ins.then_inc(zt_copy, 1)

            with act.Fori(0, 4) as i:
                for j in range(2):
                    for g, (c0, c1) in enumerate(GROUPS):
                        k = 3 * j + g
                        act.wait_ge(g_done, 6 * i + (G_GATE + k + 1))
                        act.wait_ge(g_free, 6 * i + (F_GATE + k))
                        nc.scalar.activation(tmp[3][:, 0:c1 - c0], ps[:, k, 0:c1 - c0],
                                             ACT.Silu).then_inc(g_act, 1)
                        if g == 0:
                            in_loop(i, I_GATE + 1 + j)
                        act.wait_ge(g_free, 6 * i + (F_GATE + k + 1))
                        nc.scalar.activation(y_hi[:, 2 * i + j, c0:c1], tmp[2][:, 0:c1 - c0],
                                             ACT.Copy).then_inc(g_high, 1)
            act.wait_ge(g_low, 24)
            for n0, u0, free0 in ((I_M1, G_M1, F_M1), (I_M2, G_M2, F_M2)):
                with act.Fori(0, 8) as i:
                    for g, (c0, c1) in enumerate(GROUPS):
                        act.wait_ge(g_done, 6 * i + (u0 + g + 1))
                        act.wait_ge(g_free, 3 * i + (free0 - 2 + g))
                        nc.scalar.activation(tmp[g][:, 0:c1 - c0], ps[:, g, 0:c1 - c0],
                                             ACT.Sigmoid).then_inc(g_act, 1)
                        if g == 0:
                            in_loop(i, n0 + 1)
                    act.wait_ge(g_done, 6 * i + (u0 + 4))
                    in_loop(i, n0 + 2)
            act.wait_ge(g_done, G_OUT)
            act.wait_ge(m_add, 24)
            for t in range(KT):
                nc.scalar.activation(xn_hi[:, t, :], res[:, t, :], ACT.Copy).then_inc(split_hi, 1)

            def residual_squares(i, j, g, c0, c1, free0, sum0):
                k = 3 * j + g
                act.wait_ge(g_free, 6 * i + (free0 + k + 1))
                act.wait_ge(summed, 6 * i + (sum0 + k - 1))
                nc.scalar.activation(tmp[4 + k % 2][:, 0:c1 - c0], res[:, 2 * i + j, c0:c1],
                                     ACT.Square).then_inc(squared, 1)

            with act.Fori(0, 4) as i:
                for j in range(2):
                    for g, (c0, c1) in enumerate(GROUPS):
                        if g == 0:
                            act.wait_ge(g_done, 6 * i + (G_OUT + 3 * j + 1))
                            in_loop(i, I_OUT + 1 + j)
                        residual_squares(i, j, g, c0, c1, F_OUT, SUM_OUT)
            roots(3, D_MODEL)
            for t in range(KT):
                act.wait_ge(scaled, KT + 6 + t + 1)
                nc.scalar.activation(xn_hi[:, t, :], norm_f[t % 2][:, :], ACT.Copy).then_inc(norm_high, 1)
            n0, u0, free0, sum0 = I_FFN, G_FFN, F_FFN, SUM_FIN
            for f, (_, tiles) in enumerate(FFN_GROUPS):
                with act.Fori(0, tiles) as i:
                    for g, (c0, c1) in enumerate(GROUPS):
                        act.wait_ge(g_done, 6 * i + (u0 + g + 1))
                        act.wait_ge(g_free, 3 * i + (free0 - 2 + g))
                        nc.scalar.activation(tmp[g][:, 0:c1 - c0], ps[:, g, 0:c1 - c0],
                                             ACT.Silu).then_inc(g_act, 1)
                        if g == 0:
                            in_loop(i, n0 + 1)
                    act.wait_ge(g_done, 6 * i + (u0 + 4))
                    in_loop(i, n0 + 2)
                    for g, (c0, c1) in enumerate(GROUPS):
                        act.wait_ge(g_free, 3 * i + (free0 + g + 1))
                        nc.scalar.activation(y_hi[:, i, c0:c1], tmp[3 + g % 2][:, 0:c1 - c0],
                                             ACT.Copy).then_inc(g_high, 1)
                n0, u0, free0 = n0 + 2 * tiles, u0 + 6 * tiles, free0 + 3 * tiles
                last_group = f == len(FFN_GROUPS) - 1

                def down(i, j, split):
                    for g, (c0, c1) in enumerate(GROUPS):
                        if g == 0 and split:
                            act.wait_ge(g_done, 6 * i + (u0 + 3 * j + 1))
                            in_loop(i, n0 + 1 + j)
                        if last_group:
                            residual_squares(i, j, g, c0, c1, free0, sum0)

                with act.Fori(0, 3 if last_group else 4) as i:
                    for j in range(2):
                        down(i, j, True)
                if last_group:
                    down(3, 0, True)
                    down(3, 1, False)
                n0, u0, free0 = n0 + 8, u0 + 24, free0 + 24
            roots(4, D_MODEL)

        @block.vector
        def _(dve):
            chained = [0]

            def chain(ins):
                chained[0] += 1
                ins.then_inc(v_chain, 1)
                dve.wait_ge(v_chain, chained[0])

            def split_low(slot, n):
                dve.wait_ge(w_high, n + 1)
                first = full_blocks(n) if isinstance(n, int) else 0
                nc.vector.tensor_tensor(w_lo[:, slot, first:8, :], stage[slot][:, first:8, :],
                                        w_hi[:, slot, first:8, :].bitcast(F32), ALU.subtract).then_inc(w_low, 1)

            def item(n):
                split_low(n % 2, n)

            def in_loop(i, n):
                split_low(n % 2, 2 * i + n)

            def low(dst, full, high):
                return nc.vector.tensor_tensor(dst, full, high.bitcast(F32), ALU.subtract)

            def sums(first, tiles):
                for t in range(tiles):
                    k = first + t
                    dve.wait_ge(squared, k + 1)
                    if t:
                        dve.wait_ge(summed, k)
                        ins = nc.vector.tensor_tensor(sumsq[:, :], sumsq[:, :], square[:, k % 2, :], ALU.add)
                    else:
                        ins = nc.vector.tensor_copy(sumsq[:, :], square[:, k % 2, :])
                    ins.then_inc(summed, 1)

            def inverses(k, dst):
                for g, (c0, c1) in enumerate(GROUPS):
                    m = 3 * k + g
                    dve.wait_ge(root_done, m + 1)
                    nc.vector.reciprocal(dst[:, c0:c1], root[m % 2][:, 0:c1 - c0]).then_inc(inv_done, 1)
                dve.wait_ge(inv_done, 3 * k + 3)

            def odd_low(k, dst, src, high):
                dve.wait_ge(norm_high, k + 1)
                low(dst, src, high).then_inc(norm_low[1], 1)

            def normalise(src, dst, gain, inverse):
                nc.vector.scalar_tensor_tensor(dst, src, gains[:, gain:gain + 1], inverse[:, :],
                                               ALU.mult, ALU.mult).then_inc(scaled, 1)

            def swap_products(out, bank, width, rows, sin, c0, c1):
                half_rows = rows[1]
                for r in range(0, rows[0], 2 * half_rows):
                    for x, y in ((r, r + half_rows), (r + half_rows, r)):
                        last = nc.vector.tensor_tensor(out[x:x + half_rows, 0:width],
                                                       ps[y:y + half_rows, bank, 0:width],
                                                       sin[y:y + half_rows, c0:c1], ALU.mult)
                return last

            def rotate(r, bank, rows, half_rows, cos, sin, c0, c1, freed):
                if r:
                    dve.wait_ge(rot_sum, r)
                nc.vector.tensor_tensor(rot_cos[0:rows, 0:c1 - c0], ps[0:rows, bank, 0:c1 - c0],
                                        cos[0:rows, c0:c1], ALU.mult)
                swap_products(rot_sin, bank, c1 - c0, (rows, half_rows), sin, c0, c1).then_inc(freed, 1)

            nc.vector.memset(ones[:, :], 1.0)
            nc.vector.memset(half[:, :], -0.5)
            nc.vector.memset(eps[:, :], EPS).then_inc(set_up, 1)
            sums(0, KT)
            inverses(0, inv)
            dve.wait_ge(consts_in, 64)
            item(0)
            for t in range(KT):
                normalise(xt[:, t, :], xt[:, t, :], G_MIX + t, inv)
                if t >= 2 and t % 2 == 0:
                    odd_low(t - 1, xa_lo[:, t - 1, :], xt[:, t - 1, :], xa_hi[:, t - 1, :])
            odd_low(KT - 1, xa_lo[:, KT - 1, :], xt[:, KT - 1, :], xa_hi[:, KT - 1, :])

            def query_norm(t):
                normalise(cq_raw[:, t, :], cq_raw[:, t, :], G_Q + t, inv)

            def query_low(t):
                odd_low(KT + t, cqn_lo[:, t, :], cq_raw[:, t, :], cqn_hi[:, t, :])

            for j in range(N_A):
                bank = 3 * (j % 2)
                if j == 4:
                    dve.wait_ge(stat_done, 3)
                    sums(KT, 4)
                if j == 5:
                    dve.wait_ge(scaled, KT)
                    inverses(1, inv)
                    query_norm(0)
                    query_norm(1)
                for g, (c0, c1) in enumerate(GROUPS):
                    dve.wait_ge(g_done, G_A + 3 * j + g + 1)
                    if j < N_A - 1:
                        dst = cq_raw[:, j, c0:c1] if j < 4 else ckv_raw[:, j - 4, c0:c1]
                        nc.vector.tensor_copy(dst, ps[:, bank + g, 0:c1 - c0]).then_inc(g_free, 1)
                    else:
                        if g == 0:
                            dve.wait_ge(tables_in, 32)
                        rotate(g, bank + g, ROPE, ROPE // 2, cos64, sin64, c0, c1, g_free)
                    if g == 0:
                        item(I_A + j + 1)
                    if j == 5 and g == 0:
                        query_norm(2)
                        query_norm(3)
                        query_low(1)
                    if j == 5 and g == 2:
                        query_low(3)
                        sums(KT + 4, 2)
                    if j == 6 and g == 0:
                        dve.wait_ge(scaled, KT + 4)
                        inverses(2, inv)
                        for t in range(2):
                            normalise(ckv_raw[:, t, :], ckn[:, t, 0:TOK], G_KV + t, inv)

            def shared_key():
                for g, (c0, c1) in enumerate(GROUPS):
                    dve.wait_ge(rot_high, g + 1)
                    low(kp_lo[0:ROPE, c0:c1], kpe_out[0:ROPE, c0:c1], kp_hi[0:ROPE, c0:c1])
                    low(kp_lo[ROPE:P, c0:c1], kpe_out[0:ROPE, c0:c1], kp_hi[0:ROPE, c0:c1]).then_inc(rot_low, 1)
                dve.wait_ge(cache_high, 1)
                low(kp_lo[0:ROPE, TOK:KEYS], cpe_in[0:ROPE, :], kp_hi[0:ROPE, TOK:KEYS])
                low(kp_lo[ROPE:P, TOK:KEYS], cpe_in[0:ROPE, :], kp_hi[0:ROPE, TOK:KEYS]).then_inc(cache_low, 1)

            def projection(h, kind, g):
                b, key = h % 2, ("M", h, kind, g)
                u = p_order[key]
                bank = 6 + u % 2
                n = mla_item(h, kind)
                if kind == "R":
                    r = rot_index[key]
                    c0, c1 = GROUPS[g]
                    dve.wait_ge(p_done, u + 1)
                    rotate(r, bank, P, ROPE // 2, cos64, sin64, c0, c1, p_free)
                    return
                dve.wait_ge(p_high, high_index[key] + 1)
                if kind == "K":
                    c0, c1 = KEY_GROUPS[g]
                    low(k_lo[b][:, c0:c1], ps[:, bank, 0:c1 - c0], k_hi[b][:, c0:c1]).then_inc(p_free, 1)
                    if g == 0:
                        item(n + 1)
                elif kind == "V":
                    full = 4 if g < 2 else 2
                    ins = low(v_lo[b][:, 4 * g:4 * g + full, :],
                              ps[:, bank, 0:full * P].rearrange("p (t e) -> p t e", t=full),
                              v_hi[b][:, 4 * g:4 * g + full, :])
                    if g == 2:
                        ins = low(v_lo[b][0:DEC, 10, :], ps[0:DEC, bank, 256:384], v_hi[b][0:DEC, 10, :])
                    ins.then_inc(p_free, 1)
                    if g == NG - 1 and h % 2 == 0:
                        item(n + 2)
                else:
                    c0, c1 = GROUPS[g]
                    low(q_lo[b][:, c0:c1], ps[:, bank, 0:c1 - c0], q_hi[b][:, c0:c1]).then_inc(p_free, 1)

            def rotary_parts(h, g):
                c0, c1 = GROUPS[g]
                w = c1 - c0
                rotary = qr[(h // 2 + 1) % 2]
                dve.wait_ge(rot_high, rot_index["M", h, "R", g] + 1)
                low(rotary[0][64:128, c0:c1], rot_total[0:64, 0:w], rotary[0][0:64, c0:c1])
                low(rotary[1][0:64, c0:c1], rot_total[64:128, 0:w], rotary[1][64:128, c0:c1])\
                    .then_inc(rot_low, 1)

            def ret_projection(h, kind, g):
                b, key = h % 2, ("R", h, kind, g)
                u = p_order[key]
                bank = 6 + u % 2
                n = ret_item(h, kind)
                if h == 0 and kind == "Q" and g == 0:
                    dve.wait_ge(tables_in, 64)
                dve.wait_ge(p_done, u + 1)
                if kind in "QK":
                    c0, c1 = GROUPS[g]
                    rotate(rot_index[key], bank, P, DK // 2, cos128, sin128, c0, c1, p_free)
                    if g == 0:
                        item(n + 1)
                    if kind == "K" and g == NG - 1:
                        item(n + 2)
                else:
                    L = P if g < 8 else DEC
                    nc.vector.tensor_copy(rv[b][0:L, g, :], ps[0:L, bank, 0:DV]).then_inc(p_free, 1)
                    if g == 8:
                        item(n + 2)

            def fill(what, h, kind, g):
                (projection if what == "M" else ret_projection)(h, kind, g)

            for kind in "KQRV":
                for g in range(NG):
                    projection(0, kind, g)
                    if kind == "R":
                        rotary_parts(0, g)
                if kind == "K":
                    shared_key()
            for head in range(MH):
                for s in attention_steps(head):
                    if s[0] == "F":
                        fill(*s[1:])
                        continue
                    h, tile = s[1:]
                    if s[0] == "D":
                        rotary_parts(*s[1:])
                    elif s[0] == "S":
                        n = s_index(h, tile)
                        _, nk, nq = keys_of(tile)
                        bank = 2 * (n % 2)
                        scores = ps[0:nq, bank:bank + 2, :].rearrange("p b k -> p (b k)")
                        dve.wait_ge(s_done, n + 1)
                        if tile < 8:
                            chain(nc.vector.memset(scores[0:64, nk - 64:nk], NEG))
                        chain(nc.vector.reduce_max(negmax[0:nq, n % 2, 1:2], scores[:, 0:nk], AX.X))
                        nc.vector.tensor_scalar(negmax[0:nq, n % 2, 0:1], negmax[0:nq, n % 2, 1:2],
                                                -SCALE, None, ALU.mult).then_inc(max_done, 1)
                    elif s[0] == "P":
                        n = s_index(h, tile)
                        _, nk, nq = keys_of(tile)
                        dve.wait_ge(exp_done, n + 1)
                        chain(nc.vector.reciprocal(rowsum[0:nq, n % 2, 1:2], rowsum[0:nq, n % 2, 0:1]))
                        nc.vector.tensor_scalar(p_exp[n % 2][0:nq, 0:nk], p_exp[n % 2][0:nq, 0:nk],
                                                rowsum[0:nq, n % 2, 1:2], None, ALU.mult).then_inc(prob_done, 1)
                    elif s[0] == "T":
                        n = s_index(h, tile)
                        _, nk, nq = keys_of(tile)
                        q0 = P * (tile % 2) if tile < 8 else P
                        for i, (k0, nb) in enumerate(t_blocks(tile)):
                            t = t_index(h, tile) + i
                            dve.wait_ge(t_high, t + 1)
                            full = nb if tile < 8 else 2
                            src = ps[:, 4 + t % 2, 0:full * P].rearrange("p (k q) -> p k q", k=full)[:, :, 0:nq]
                            ins = low(pt_lo[:, k0:k0 + full, q0:q0 + nq], src, pt_hi[:, k0:k0 + full, q0:q0 + nq])
                            if tile == 8:
                                ins = low(pt_lo[0:DEC, 2, q0:q0 + nq], ps[0:DEC, 4 + t % 2, 2 * P:2 * P + nq],
                                          pt_hi[0:DEC, 2, q0:q0 + nq])
                            ins.then_inc(t_low, 1)
                    elif s[0] == "O":
                        pair = s[2]
                        n = o_index(h, pair)
                        w = DEC if pair == 4 else 2 * P
                        u = p_order["M", h, "O", pair]
                        dve.wait_ge(p_high, high_index["M", h, "O", pair] + 1)
                        low(out_hl[n % 2][:, 1, 0:w], ps[:, 6 + u % 2, 0:w],
                            out_hl[n % 2][:, 0, 0:w]).then_inc(p_free, 1)

            for h in range(RH):
                gamma = 1.0 - 2.0 ** (-5.0 - h)
                for s in retention_steps(h):
                    if s[0] == "F":
                        fill(*s[1:])
                        continue
                    c = s[1]
                    n = 9 * h + c
                    L = P if c < 8 else DEC
                    if s[0] == "A":
                        dve.wait_ge(sc_done, n + 1)
                        if n >= 2:
                            dve.wait_ge(z_done, n - 1)
                        nc.vector.tensor_tensor(st_f[n % 2][0:L, 0:L], ps[0:L, 0, 0:L], dmask[0:L, h, 0:L],
                                                ALU.mult).then_inc(sc_mid, 1)
                    elif s[0] == "B":
                        state = s_prompt[h % 2] if c < 8 else s_sample[h % 2]
                        dve.wait_ge(u_done, n + 1)
                        nc.vector.scalar_tensor_tensor(state[:, :], state[:, :], gamma ** L, ps[:, 4, 0:DV],
                                                       ALU.mult, ALU.add).then_inc(state_f, 1)
                        dve.wait_ge(z_copy, n + 1)
                        chain(nc.vector.bn_stats(bnst[0:L, n % 2, :], zs[n % 2][0:L, :]))
                        nc.vector.bn_aggr(mv[0:L, n % 2, :], bnst[0:L, n % 2, :]).then_inc(z_stat, 1)
                    elif s[0] == "N":
                        dve.wait_ge(z_rstd, n + 1)
                        if n >= 2:
                            dve.wait_ge(zt_done, n - 1)
                        nc.vector.tensor_scalar(zn[n % 2][0:L, :], zs[n % 2][0:L, :], mv[0:L, n % 2, 0:1],
                                                rstd[0:L, n % 2, :], ALU.subtract, ALU.mult).then_inc(z_norm, 1)

            with dve.Fori(0, 4) as i:
                for j in range(2):
                    for g, (c0, c1) in enumerate(GROUPS):
                        k = 3 * j + g
                        w = c1 - c0
                        dve.wait_ge(g_act, 6 * i + (k + 1))
                        dve.wait_ge(yr_in[k % 2], 48 * i + 16 * (k // 2 + 1))
                        nc.vector.tensor_tensor(tmp[2][:, 0:w], tmp[3][:, 0:w], tmp[k % 2][:, 0:w],
                                                ALU.mult).then_inc(g_free, 1)
                        if g == 0:
                            in_loop(i, I_GATE + 1 + j)
                        dve.wait_ge(g_high, 6 * i + (k + 1))
                        low(y_lo[:, 2 * i + j, c0:c1], tmp[2][:, 0:w], y_hi[:, 2 * i + j, c0:c1]).then_inc(g_low, 1)
                        dve.wait_ge(g_low, 6 * i + (k + 1))
            for b in range(2):
                dve.wait_ge(state_out[b], 16 * RH)
            for n0, u0, act0, free0 in ((I_M1, G_M1, A_M1, F_M1), (I_M2, G_M2, A_M2, F_M2)):
                with dve.Fori(0, 8) as i:
                    in_loop(i, n0 + 1)
                    for g, (c0, c1) in enumerate(GROUPS):
                        w = c1 - c0
                        dve.wait_ge(g_act, 3 * i + (act0 + g + 1))
                        dve.wait_ge(g_done, 6 * i + (u0 + 3 + g + 1))
                        dst = tmp[3 + g][:, 0:w] if n0 == I_M2 else res[:, i, c0:c1]
                        nc.vector.tensor_tensor(dst, ps[:, 3 + g, 0:w], tmp[g][:, 0:w], ALU.mult)\
                          .then_inc(g_free, 1)
                        if g == 0:
                            in_loop(i, n0 + 2)
                        if n0 == I_M2:
                            dve.wait_ge(g_free, 3 * i + (free0 + g + 1))
                            nc.vector.tensor_tensor(res[:, i, c0:c1], res[:, i, c0:c1], tmp[3 + g][:, 0:w],
                                                    ALU.add).then_inc(m_add, 1)
                    if n0 == I_M2:
                        dve.wait_ge(m_add, 3 * i + 3)
            for t in range(KT):
                dve.wait_ge(split_hi, t + 1)
                low(xn_lo[:, t, :], res[:, t, :], xn_hi[:, t, :]).then_inc(split_lo, 1)
            dve.wait_ge(split_lo, KT)
            nc.vector.memset(res_sq[:, :], 0.0).then_inc(set_up, 1)
            dve.wait_ge(set_up, 2)

            def residual_sum(i, j, g, c0, c1, sum0):
                k = 3 * j + g
                dve.wait_ge(squared, 6 * i + (sum0 + k + 1))
                dve.wait_ge(summed, 6 * i + (sum0 + k - 2))
                nc.vector.tensor_tensor(res_sq[:, c0:c1], res_sq[:, c0:c1], tmp[4 + k % 2][:, 0:c1 - c0],
                                        ALU.add).then_inc(summed, 1)

            with dve.Fori(0, 4) as i:
                for j in range(2):
                    for g, (c0, c1) in enumerate(GROUPS):
                        k = 3 * j + g
                        w = c1 - c0
                        dve.wait_ge(g_done, 6 * i + (G_OUT + k + 1))
                        dve.wait_ge(xres_in[k % 2], 48 * i + 16 * (k // 2 + 1))
                        nc.vector.tensor_tensor(res[:, 2 * i + j, c0:c1], ps[:, k, 0:w], tmp[k % 2][:, 0:w],
                                                ALU.add).then_inc(g_free, 1)
                        if g == 0:
                            in_loop(i, I_OUT + 1 + j)
                        residual_sum(i, j, g, c0, c1, SUM_OUT)
            inverses(3, res_inv)

            def residual_low(t):
                odd_low(KT + 4 + t, xn_lo[:, t, :], norm_f[t % 2][:, :], xn_hi[:, t, :])

            for t in range(KT):
                if t >= 2:
                    wait_low(dve, KT + 4 + t - 2)
                normalise(res[:, t, :], norm_f[t % 2][:, :], G_F + t, res_inv)
                if t >= 2 and t % 2 == 0:
                    residual_low(t - 1)
            residual_low(KT - 1)
            dve.wait_ge(stat_done, 12)
            n0, u0, act0, free0, low0 = I_FFN, G_FFN, A_FFN, F_FFN, 24
            for f, (_, tiles) in enumerate(FFN_GROUPS):
                with dve.Fori(0, tiles) as i:
                    in_loop(i, n0 + 1)
                    for g, (c0, c1) in enumerate(GROUPS):
                        w = c1 - c0
                        dve.wait_ge(g_act, 3 * i + (act0 + g + 1))
                        dve.wait_ge(g_done, 6 * i + (u0 + 3 + g + 1))
                        if g == 2:
                            dve.wait_ge(g_low, 3 * i + (low0 + 1))
                        nc.vector.tensor_tensor(tmp[3 + g % 2][:, 0:w], ps[:, 3 + g, 0:w], tmp[g][:, 0:w],
                                                ALU.mult).then_inc(g_free, 1)
                        if g == 0:
                            in_loop(i, n0 + 2)
                        dve.wait_ge(g_high, 3 * i + (low0 + g + 1))
                        low(y_lo[:, i, c0:c1], tmp[3 + g % 2][:, 0:w], y_hi[:, i, c0:c1]).then_inc(g_low, 1)
                    dve.wait_ge(g_low, 3 * i + (low0 + 3))
                n0, u0 = n0 + 2 * tiles, u0 + 6 * tiles
                act0, free0, low0 = act0 + 3 * tiles, free0 + 3 * tiles, low0 + 3 * tiles
                last_group = f == len(FFN_GROUPS) - 1
                if last_group:
                    nc.vector.memset(res_sq[:, :], 0.0).then_inc(set_up, 1)
                    dve.wait_ge(set_up, 3)

                def down(i, j, split):
                    for g, (c0, c1) in enumerate(GROUPS):
                        k = 3 * j + g
                        dve.wait_ge(g_done, 6 * i + (u0 + k + 1))
                        nc.vector.tensor_tensor(res[:, 2 * i + j, c0:c1], res[:, 2 * i + j, c0:c1],
                                                ps[:, k, 0:c1 - c0], ALU.add).then_inc(g_free, 1)
                        if g == 0 and split:
                            in_loop(i, n0 + 1 + j)
                        if last_group:
                            residual_sum(i, j, g, c0, c1, SUM_FIN)

                with dve.Fori(0, 3 if last_group else 4) as i:
                    for j in range(2):
                        down(i, j, True)
                if last_group:
                    down(3, 0, True)
                    down(3, 1, False)
                n0, u0, free0 = n0 + 8, u0 + 24, free0 + 24
            inverses(4, res_inv)
            for t in range(KT):
                normalise(res[:, t, :], res[:, t, :], G_FIN + t, res_inv)

        @block.gpsimd
        def _(pool):
            def lows(first, dst, src, high, tiles):
                for t in range(0, tiles, 2):
                    pool.wait_ge(norm_high, first + t + 1)
                    nc.gpsimd.tensor_tensor(dst(t), src(t), high(t).bitcast(F32), ALU.subtract)\
                      .then_inc(norm_low[0], 1)

            def add_products(r, dst, rows, width, freed, count):
                pool.wait_ge(freed, count)
                if NG < r < ROT_MLA:
                    pool.wait_ge(rot_low, r)
                nc.gpsimd.tensor_tensor(dst, rot_cos[0:rows, 0:width], rot_sin[0:rows, 0:width],
                                        ALU.add).then_inc(rot_sum, 1)

            lows(0, lambda t: xa_lo[:, t, :], lambda t: xt[:, t, :], lambda t: xa_hi[:, t, :], KT)
            lows(KT, lambda t: cqn_lo[:, t, :], lambda t: cq_raw[:, t, :], lambda t: cqn_hi[:, t, :], 4)
            for g, (c0, c1) in enumerate(GROUPS):
                add_products(g, kpe_out[0:ROPE, c0:c1], ROPE, c1 - c0, g_free, 3 * (N_A - 1) + g + 1)

            def fill(what, h, kind, g):
                key = (what, h, kind, g)
                if key in rot_index:
                    c0, c1 = GROUPS[g]
                    total = {"R": rot_total, "Q": rq[h % 2], "K": rk[h % 2]}[kind]
                    dst = total[:, 0:c1 - c0] if kind == "R" else total[:, c0:c1]
                    add_products(rot_index[key], dst, P, c1 - c0, p_free, p_order[key] + 1)

            for g in range(NG):
                fill("M", 0, "R", g)
            for h in range(MH):
                if h:
                    pool.wait_ge(p_done, p_order["M", h - 1, "O", 3] + 1)
                else:
                    pool.wait_ge(scaled, KT + 6)
                    wait_low(pool, KT + 3)
                nc.gpsimd.memset(pt_hi[:, 1:8:2, 0:P].bitcast(F32), 0.0)
                nc.gpsimd.memset(pt_lo[:, 1:8:2, 0:P].bitcast(F32), 0.0).then_inc(pt_zero, 1)
                for s in attention_steps(h):
                    if s[0] == "F":
                        fill(*s[1:])

            pool.wait_ge(p_free, ATT_END)
            for h in range(RH):
                if h >= 2:
                    pool.wait_ge(state_out[h % 2], 32 * (h // 2))
                nc.gpsimd.memset(s_prompt[h % 2][:, :], 0.0).then_inc(state_zero, 1)
                for s in retention_steps(h):
                    if s[0] == "F":
                        fill(*s[1:])
                    elif s[0] == "B":
                        n = 9 * h + s[1]
                        L = P if s[1] < 8 else DEC
                        pool.wait_ge(z_stat, n + 1)
                        nc.gpsimd.tensor_scalar(veps[0:L, n % 2, :], mv[0:L, n % 2, 1:2], EPS, None, ALU.add)\
                          .then_inc(pool_chain, 1)
                        pool.wait_ge(pool_chain, n + 1)
                        nc.gpsimd.tensor_tensor(rstd[0:L, n % 2, :], veps[0:L, n % 2, :], half[0:L, :],
                                                ALU.pow).then_inc(z_rstd, 1)
            lows(KT + 4, lambda t: xn_lo[:, t, :], lambda t: norm_f[t % 2][:, :], lambda t: xn_hi[:, t, :], KT)


def kernel(**inputs):
    import numpy as np
    import concourse.bacc as bacc
    from concourse.bass_utils import run_bass_kernel_spmd

    f32 = np.float32

    def feature_major(x):
        return np.ascontiguousarray(x.T.reshape(-1, P, x.shape[0]).transpose(1, 0, 2))

    def blocks(w, rows, cols):
        return w[:rows * P][:, cols].reshape(rows, P, -1).transpose(1, 0, 2)

    w_in = np.asarray(inputs["w_in"][0])
    w_uq, w_ukv = np.asarray(inputs["w_uq"][0]), np.asarray(inputs["w_ukv"][0])
    w_gu, w_down = np.asarray(inputs["w_gate_up"][0]), np.asarray(inputs["w_down"][0])
    offs = np.cumsum([0, RH * DK, RH * DK, RH * DV, RH * DV, Q_LORA, KV_LORA, ROPE, D_MODEL, D_MODEL])
    o_rq, o_rk, o_rv, o_rg, o_cq, o_ckv, o_kpe, o_ga, o_gb = offs[:9].tolist()

    W = np.zeros((N_ITEMS, P, 8, P), f32)
    n = [0]

    def put(*parts):
        k = 0
        for part in parts:
            W[n[0], :, k:k + part.shape[1], 0:part.shape[2]] = part
            k += part.shape[1]
        n[0] += 1

    def col(start, width=P):
        return slice(start, start + width)

    for start in [o_cq + P * t for t in range(4)] + [o_ckv, o_ckv + P]:
        put(blocks(w_in, KT, col(start)))
    put(blocks(w_in, KT, col(o_kpe, ROPE)))
    hq = NOPE + ROPE
    for h in range(MH):
        put(blocks(w_ukv, 2, col(h * (NOPE + VD))), blocks(w_ukv, 2, col(h * (NOPE + VD) + NOPE)),
            blocks(w_uq, 4, col(h * hq)))
        if h % 2 == 0:
            put(blocks(w_uq, 4, np.r_[h * hq + NOPE:(h + 1) * hq, (h + 1) * hq + NOPE:(h + 2) * hq]))
    for h in range(RH):
        put(blocks(w_in, KT, col(o_rq + P * h)))
        put(blocks(w_in, KT, col(o_rk + P * h)))
        halves = [col(o_rv + DV * h), col(o_rv + DV * h + P)]
        for half in (halves if n[0] % 2 == 0 else halves[::-1]):
            put(blocks(w_in, KT, half))
    for t in range(8):
        put(blocks(w_in, KT, col(o_rg + P * t)))
    for gate, w in ((o_ga, inputs["w_ret_o"][0]), (o_gb, inputs["w_mla_o"][0])):
        w = np.asarray(w)
        for t in range(KT):
            put(blocks(w_in, KT, col(gate + P * t)))
            put(blocks(w, KT, col(P * t)))
    for t in range(KT):
        put(blocks(np.asarray(inputs["w_out"][0]), KT, col(P * t)))
    for first, tiles in FFN_GROUPS:
        for t in range(first, first + tiles):
            put(blocks(w_gu, KT, col(P * t)))
            put(blocks(w_gu, KT, col(D_FF + P * t)))
        for t in range(KT):
            put(blocks(w_down[first * P:], tiles, col(P * t)))
    assert n[0] == N_ITEMS

    pos = np.concatenate([np.arange(SEQ), PAST + np.arange(DEC)]).astype(f32)

    def rotation(d):
        inv = (f32(10000.0) ** (-np.arange(0, d, 2, dtype=f32) / f32(d))).astype(f32)
        ang = pos[None, :] * inv[:, None]
        cos, sin = np.cos(ang), np.sin(ang)
        reps = P // d
        return (np.tile(np.concatenate([cos, cos]), (reps, 1)).astype(f32),
                np.tile(np.concatenate([sin, -sin]), (reps, 1)).astype(f32))

    cos64, sin64 = rotation(ROPE)
    cos128, sin128 = rotation(DK)
    row = np.arange(P, dtype=np.float64)
    dmask = np.zeros((P, RH, P), f32)
    dcol = np.zeros((P, RH, 3), f32)
    for h in range(RH):
        gamma = 1.0 - 2.0 ** (-5.0 - h)
        dmask[:, h, :] = np.where(row[None, :] >= row[:, None], gamma ** -(row[:, None] + 1), 0.0) * DK ** -0.5
        dcol[:, h, 0] = gamma ** (row + 1)
        dcol[:, h, 1] = gamma ** (P - 1 - row) * DK ** -0.5
        dcol[:DEC, h, 2] = gamma ** (DEC - 1 - row[:DEC]) * DK ** -0.5

    def gain(name):
        return np.asarray(inputs[name]).reshape(-1, P).T

    arrays = {
        "weights": W,
        "x": feature_major(np.concatenate([inputs["x_prompt"][0], inputs["x_sample"][0]])),
        "cache_ckv": feature_major(np.asarray(inputs["cache_ckv"][0, 0])),
        "cache_kpe": np.ascontiguousarray(np.asarray(inputs["cache_kpe"][0, 0]).T),
        "state": np.ascontiguousarray(np.asarray(inputs["state_ret"][0, 0]).transpose(1, 0, 2)),
        "gains": np.ascontiguousarray(np.concatenate(
            [gain(k) for k in ("norm_mix_w", "q_norm_w", "kv_norm_w", "ret_gn_w", "norm_ffn_w", "norm_final_w")],
            axis=1)),
        "eye": np.eye(P, dtype=f32),
        "cos64": cos64, "sin64": sin64, "cos128": cos128, "sin128": sin128, "dmask": dmask, "dcol": dcol,
    }
    nc = bacc.Bacc("TRN2", target_bir_lowering=False, num_devices=1)
    ins = {k: nc.dram_tensor(f"in_{k}", v.shape, F32, kind="ExternalInput").ap() for k, v in arrays.items()}
    shapes = {"y": (P, KT, TOK), "ckv": (P, 2, TOK), "kpe": (ROPE, TOK),
              "state_p": (P, RH, DV), "state_s": (P, RH, DV)}
    outs = {k: nc.dram_tensor(f"out_{k}", v, F32, kind="ExternalOutput").ap() for k, v in shapes.items()}
    build(nc, ins, outs)
    run = run_bass_kernel_spmd(nc, [{f"in_{k}": v for k, v in arrays.items()}], core_ids=[0])
    got = {k: run.results[0][f"out_{k}"] for k in shapes}

    def token_major(x):
        return np.ascontiguousarray(x.transpose(2, 1, 0).reshape(x.shape[2], -1))

    y, ckv = token_major(got["y"]), token_major(got["ckv"])
    kpe = np.ascontiguousarray(got["kpe"].T)
    state = [np.ascontiguousarray(got[k].transpose(1, 0, 2))[None, None] for k in ("state_p", "state_s")]
    return (y[None, :SEQ], y[None, SEQ:], ckv[None, None, :SEQ], kpe[None, None, :SEQ], state[0],
            ckv[None, None, SEQ:], kpe[None, None, SEQ:], state[1])
```
